# Optimizing a Trainium2 kernel written in Bass

```python
import math
import jax, jax.numpy as jnp
from jax import lax
import numpy as np

D_MODEL = 1024
BATCH = 1
SEQ = 256
DEPTH = 1
DEC_BATCH = 1
DEC_SEQ = 1024
PAST_LEN = 512

GRID_W = 64
D_CONV = 512
CONV_WIDTH = 31
N_HEADS_NA = 8
HEAD_DIM = 64
D_ATTN = N_HEADS_NA * HEAD_DIM
NA_ROWS_MAX = 8
NA_COLS = 16
N_EXPERTS = 16
D_EXPERT = 2048
EC_CAPACITY = 2
N_MOD = 6
EPS = 1e-6
D_IN = 2 * D_CONV + 3 * D_ATTN + 2 * D_MODEL

kernel_name = "hybrid_conformer_natten_ec_diffusion_step"

def rms_norm(x, g):
    xf = x.astype(jnp.float32)
    xf = xf * lax.rsqrt(jnp.mean(xf * xf, axis=-1, keepdims=True) + EPS)
    return (xf * g.astype(jnp.float32)).astype(x.dtype)

def layer_norm(x, g, b):
    xf = x.astype(jnp.float32)
    mu = jnp.mean(xf, axis=-1, keepdims=True)
    var = jnp.mean(jnp.square(xf - mu), axis=-1, keepdims=True)
    y = (xf - mu) * lax.rsqrt(var + EPS)
    return (y * g.astype(jnp.float32) + b.astype(jnp.float32)).astype(x.dtype)

def ada_modulation(cond, w_ada, b_ada):
    m = jax.nn.silu(cond) @ w_ada + b_ada
    return jnp.split(m[:, None, :], N_MOD, axis=-1)

def modulate(h, shift, scale):
    return h * (1 + scale) + shift

def combined_projection(h, w_in):
    B, T, _ = h.shape
    u = h @ w_in
    conv_in = u[..., :2 * D_CONV]
    qkv = u[..., 2 * D_CONV:2 * D_CONV + 3 * D_ATTN].reshape(B, T, 3, N_HEADS_NA, HEAD_DIM)
    gates = jax.nn.sigmoid(u[..., 2 * D_CONV + 3 * D_ATTN:])
    return conv_in, qkv[:, :, 0], qkv[:, :, 1], qkv[:, :, 2], gates

def conformer_conv_branch(u, dw_w, dw_b, ln_g, ln_b, w_pw):
    val, gate = jnp.split(u, 2, axis=-1)
    v = val * jax.nn.sigmoid(gate)
    pad = CONV_WIDTH // 2
    v = lax.conv_general_dilated(
        v, dw_w[:, None, :].astype(v.dtype), window_strides=(1,), padding=[(pad, pad)],
        dimension_numbers=('NWC', 'WIO', 'NWC'), feature_group_count=D_CONV) + dw_b
    v = jax.nn.silu(layer_norm(v, ln_g, ln_b))
    return v @ w_pw

def context_attention(q, k, v):
    s = jnp.einsum('bqhd,bkhd->bhqk', q, k).astype(jnp.float32) * (HEAD_DIM ** -0.5)
    p = jax.nn.softmax(s, axis=-1).astype(v.dtype)
    return jnp.einsum('bhqk,bkhd->bqhd', p, v)

def neighbourhood_attention(q, k, v, k_ctx, v_ctx, rpb):
    B, T, H, dh = q.shape
    rows = T // GRID_W
    kh = min(NA_ROWS_MAX, rows)
    kw = NA_COLS
    n_cb = GRID_W // kw
    band_w = 2 * kw
    L = kh * band_w
    r = np.arange(rows)
    row_start = np.clip(r - kh // 2, 0, rows - kh)
    cb0 = np.arange(n_cb) * kw
    band_start = np.clip(cb0 - kw // 2, 0, GRID_W - band_w)
    key_rows = row_start[:, None] + np.arange(kh)
    key_cols = band_start[:, None] + np.arange(band_w)
    key_idx = (key_rows[:, None, :, None] * GRID_W
               + key_cols[None, :, None, :]).reshape(rows, n_cb, L)
    q_cols = cb0[:, None] + np.arange(kw)
    col_start = np.clip(q_cols - kw // 2, 0, GRID_W - kw)
    kc = np.tile(key_cols, (1, kh))
    mask = ((kc[:, None, :] >= col_start[:, :, None])
            & (kc[:, None, :] < col_start[:, :, None] + kw))
    dr = np.repeat(key_rows - r[:, None], band_w, axis=1) + NA_ROWS_MAX - 1
    dc = np.clip(kc[:, None, :] - q_cols[:, :, None], -(kw - 1), kw - 1) + kw - 1
    bias = rpb[:, dr[:, None, None, :], dc[None, :, :, :]]
    bias = jnp.transpose(bias, (1, 2, 0, 3, 4)).astype(jnp.float32)

    kg = k[:, key_idx]
    vg = v[:, key_idx]
    qb = q.reshape(B, rows, n_cb, kw, H, dh)
    scale = HEAD_DIM ** -0.5
    s_loc = jnp.einsum('brnqhd,brnlhd->brnhql', qb, kg).astype(jnp.float32) * scale + bias[None]
    s_loc = jnp.where(mask[None, None, :, None, :, :], s_loc, -jnp.inf)
    s_ctx = jnp.einsum('brnqhd,bphd->brnhqp', qb, k_ctx).astype(jnp.float32) * scale
    p = jax.nn.softmax(jnp.concatenate([s_loc, s_ctx], axis=-1), axis=-1).astype(v.dtype)
    o = (jnp.einsum('brnhql,brnlhd->brnqhd', p[..., :L], vg)
         + jnp.einsum('brnhqp,bphd->brnqhd', p[..., L:], v_ctx))
    return o.reshape(B, T, H, dh)

def merge_branches(conv_out, attn_heads, gates, w_attn_o, w_out):
    B, T, _ = conv_out.shape
    attn_out = attn_heads.reshape(B, T, D_ATTN) @ w_attn_o
    g_a, g_b = jnp.split(gates, 2, axis=-1)
    return (g_a * conv_out + g_b * attn_out) @ w_out

def expert_choice_ffn(h, w_router, w_gate, w_up, w_down):
    B, T, D = h.shape
    cap = EC_CAPACITY * T // N_EXPERTS
    aff = jax.nn.softmax((h @ w_router).astype(jnp.float32), axis=-1)
    g, idx = lax.top_k(jnp.swapaxes(aff, 1, 2), cap)
    xe = jax.vmap(lambda hb, ib: hb[ib])(h, idx)
    hid = (jax.nn.silu(jnp.einsum('becd,edf->becf', xe, w_gate))
           * jnp.einsum('becd,edf->becf', xe, w_up))
    ye = jnp.einsum('becf,efd->becd', hid, w_down) * g[..., None].astype(h.dtype)
    return jax.vmap(lambda yb, ib: jnp.zeros((T, D), yb.dtype).at[ib.reshape(-1)].add(
        yb.reshape(-1, D)))(ye, idx)

def setup_inputs(seed: int = 0) -> dict:
    key = jax.random.key(seed)
    ks = jax.random.split(key, 24)

    def nrm(k, shape, scale):
        return jax.random.normal(k, shape, jnp.float32) * scale

    L = DEPTH
    return {
        'x_prompt': nrm(ks[0], (BATCH, SEQ, D_MODEL), 1.0),
        'x_sample': nrm(ks[1], (DEC_BATCH, DEC_SEQ, D_MODEL), 1.0),
        'cache_ctx_k': nrm(ks[2], (DEC_BATCH, L, PAST_LEN, N_HEADS_NA, HEAD_DIM), 1.0),
        'cache_ctx_v': nrm(ks[3], (DEC_BATCH, L, PAST_LEN, N_HEADS_NA, HEAD_DIM), 1.0),
        'c': nrm(ks[4], (DEC_BATCH, D_MODEL), 1.0),
        'c_ctx': nrm(ks[5], (D_MODEL,), 1.0),
        'w_ada': nrm(ks[6], (L, D_MODEL, N_MOD * D_MODEL), 0.5 * D_MODEL ** -0.5),
        'b_ada': nrm(ks[7], (L, N_MOD * D_MODEL), 0.02),
        'norm1_g': 1.0 + nrm(ks[8], (L, D_MODEL), 0.02),
        'w_in': nrm(ks[9], (L, D_MODEL, D_IN), D_MODEL ** -0.5),
        'conv_dw_w': nrm(ks[10], (L, CONV_WIDTH, D_CONV), CONV_WIDTH ** -0.5),
        'conv_dw_b': nrm(ks[11], (L, D_CONV), 0.02),
        'conv_ln_g': 1.0 + nrm(ks[12], (L, D_CONV), 0.02),
        'conv_ln_b': nrm(ks[13], (L, D_CONV), 0.02),
        'w_conv_pw': nrm(ks[14], (L, D_CONV, D_MODEL), D_CONV ** -0.5),
        'na_rpb': nrm(ks[15], (L, N_HEADS_NA, 2 * NA_ROWS_MAX - 1, 2 * NA_COLS - 1), 0.1),
        'w_attn_o': nrm(ks[16], (L, D_ATTN, D_MODEL), D_ATTN ** -0.5),
        'w_out': nrm(ks[17], (L, D_MODEL, D_MODEL), D_MODEL ** -0.5),
        'norm2_g': 1.0 + nrm(ks[18], (L, D_MODEL), 0.02),
        'w_router': nrm(ks[19], (L, D_MODEL, N_EXPERTS), D_MODEL ** -0.5),
        'w_gate_e': nrm(ks[20], (L, N_EXPERTS, D_MODEL, D_EXPERT), D_MODEL ** -0.5),
        'w_up_e': nrm(ks[21], (L, N_EXPERTS, D_MODEL, D_EXPERT), D_MODEL ** -0.5),
        'w_down_e': nrm(ks[22], (L, N_EXPERTS, D_EXPERT, D_MODEL), D_EXPERT ** -0.5),
        'final_g': 1.0 + nrm(ks[23], (D_MODEL,), 0.02),
    }

def reference(x_prompt, x_sample, cache_ctx_k, cache_ctx_v, c, c_ctx, w_ada, b_ada, norm1_g,
              w_in, conv_dw_w, conv_dw_b, conv_ln_g, conv_ln_b, w_conv_pw, na_rpb, w_attn_o,
              w_out, norm2_g, w_router, w_gate_e, w_up_e, w_down_e, final_g):
    xp = x_prompt
    xs = x_sample
    new_k = []
    new_v = []
    for l in range(DEPTH):
        sh1, sc1, g1, sh2, sc2, g2 = ada_modulation(c_ctx[None, :], w_ada[l], b_ada[l])
        h = modulate(rms_norm(xp, norm1_g[l]), sh1, sc1)
        conv_in, q, k, v, gates = combined_projection(h, w_in[l])
        conv_out = conformer_conv_branch(conv_in, conv_dw_w[l], conv_dw_b[l], conv_ln_g[l],
                                         conv_ln_b[l], w_conv_pw[l])
        attn = context_attention(q, k, v)
        xp = xp + g1 * merge_branches(conv_out, attn, gates, w_attn_o[l], w_out[l])
        h = modulate(rms_norm(xp, norm2_g[l]), sh2, sc2)
        xp = xp + g2 * expert_choice_ffn(h, w_router[l], w_gate_e[l], w_up_e[l], w_down_e[l])
        new_k.append(k)
        new_v.append(v)

        sh1, sc1, g1, sh2, sc2, g2 = ada_modulation(c, w_ada[l], b_ada[l])
        h = modulate(rms_norm(xs, norm1_g[l]), sh1, sc1)
        conv_in, q, k, v, gates = combined_projection(h, w_in[l])
        conv_out = conformer_conv_branch(conv_in, conv_dw_w[l], conv_dw_b[l], conv_ln_g[l],
                                         conv_ln_b[l], w_conv_pw[l])
        attn = neighbourhood_attention(q, k, v, cache_ctx_k[:, l], cache_ctx_v[:, l], na_rpb[l])
        xs = xs + g1 * merge_branches(conv_out, attn, gates, w_attn_o[l], w_out[l])
        h = modulate(rms_norm(xs, norm2_g[l]), sh2, sc2)
        xs = xs + g2 * expert_choice_ffn(h, w_router[l], w_gate_e[l], w_up_e[l], w_down_e[l])

    y_prompt = rms_norm(xp, final_g)
    y_sample = rms_norm(xs, final_g)
    state_ctx_k = jnp.stack(new_k, axis=1)
    state_ctx_v = jnp.stack(new_v, axis=1)
    return (y_prompt, y_sample, state_ctx_k, state_ctx_v)


_drawn_inputs = setup_inputs


def setup_inputs(seed=0):
    import zlib

    import numpy as np

    out = dict(_drawn_inputs(seed))
    spreads = {}
    factors = {'cache_ctx_k': 6.553,
     'cache_ctx_v': 5.582,
     'norm1_g': 3.104,
     'conv_dw_b': 8.0,
     'conv_ln_g': 8.0,
     'conv_ln_b': 8.0,
     'na_rpb': 174.183,
     'norm2_g': 7.209,
     'final_g': 23.729}
    for name, (base, spread) in spreads.items():
        noise = np.random.default_rng([zlib.crc32(name.encode()), seed]).standard_normal(out[name].shape)
        drawn = base * np.exp(spread * noise) if base else spread * noise
        out[name] = __import__('jax').numpy.asarray(drawn.astype(out[name].dtype))
    for name, factor in factors.items():
        out[name] = (out[name] * factor).astype(out[name].dtype)
    return out
```

```python
from contextlib import ExitStack

import numpy as np

import concourse.bass as bass
from concourse import mybir

ALU = mybir.AluOpType
ACT = mybir.ActivationFunctionType
F32 = mybir.dt.float32
U32 = mybir.dt.uint32
AX_X = mybir.AxisListType.X
ds = bass.ds

P = 128
D = 1024
KD = D // P
TS, TP = 1024, 256
T = TS + TP
NT = T // P
GRID_W = 64
ROWS = TS // GRID_W
PAST = 512
DC = 512
KC = DC // P
TAPS = 31
PAD = TAPS // 2
DH = 64
HEADS = 8
NE = 16
DE = 2048
KE = DE // P
CAP_S, CAP_P = 2 * TS // NE, 2 * TP // NE
CAP = CAP_S + CAP_P
EPS = 1e-6
MASKED = -1e30
RPB_R, RPB_C = 15, 31
SLOTS = 14
TOK = [(0, 512), (512, 512), (1024, 256)]
GLU_W = TS + TP + 4 * PAD
GLU_AT = [PAD, PAD + 512, TS + 3 * PAD]
CONV_W = GLU_W - 2 * PAD
CONV_AT = [0, 512, TS + 2 * PAD]
PAIRS = []
for _r in range(0, ROWS, 2):
    _s = min(max(_r - 4, 0), ROWS - 8)
    _s2 = min(max(_r - 3, 0), ROWS - 8)
    PAIRS.append((_s, 8 if _s2 == _s else 9, _s - _r + 7))


def window_masks():
    q = np.arange(P) % GRID_W
    start = np.clip(q - 8, 0, GRID_W - 16)[:, None]
    kc = np.arange(GRID_W)[None, :]
    col = np.where((kc >= start) & (kc < start + 16), 0.0, MASKED).astype(np.float32)
    m = np.repeat(col[:, None, :], 10, axis=1)
    m[GRID_W:, 1, :] = MASKED
    m[:GRID_W, 9, :] = MASKED
    return np.ascontiguousarray(m)


def backbone(nc, A, O):
    ctx = ExitStack()
    with ctx:
        def sem(name):
            return ctx.enter_context(nc.semaphore(name))

        arena = ctx.enter_context(nc.sbuf_tensor("arena", [P, 53120], F32))

        def at(off, *dims):
            n = int(np.prod(dims))
            v = arena[:, off:off + n]
            if len(dims) == 1:
                return v
            names = "abcd"[:len(dims)]
            return v.rearrange(f"p ({' '.join(names)}) -> p {' '.join(names)}",
                               **{k: d for k, d in zip(names, dims)})

        bank = [ctx.enter_context(nc.psum_tensor(f"bank{i}", [P, 512], F32)) for i in range(8)]

        HT, CONV, GLU = 0, 10240, 15480
        Q, K, V = 21400, 26520, 31640
        R = 36760
        hT = at(HT, KD, T)
        conv = at(CONV, KC, CONV_W)
        glu = at(GLU, KC, GLU_W)
        qT = at(Q, KC, T)
        kT = at(K, KC, T)
        vtok = at(V, NT, DC)
        xin = at(K, NT, D)
        ws = [at(R + 2048 * i, KD, 256) for i in range(4)]
        sg = at(R + 8192, 2, 512)
        sq = at(R, KC, 512)
        rs = at(R + 8192, 512)
        bias = [[(at(GLU + 2944 * i + 1472 * h, SLOTS, GRID_W), at(GLU + 2944 * i + 1472 * h + 896, 9, GRID_W))
                 for h in range(2)] for i in range(2)]
        kcT = at(R, KC, PAST)
        vc = at(R + 2048, PAST // P, DC)
        S = at(R + 4096, 2, 576)
        Pr = at(R + 5248, 2, 1088)
        PT = at(R + 7424, 2, 1152)
        qz = at(R + 9728, 4, P)
        kraw = at(R + 4096, PAST // P, DC)
        kst = at(R + 6144, 2, DC)
        merged = at(K, KD, T)
        wm = [at(R + 3072 * i, 24, P) for i in range(2)]
        gs = at(R + 6144, 2, 2, 512)
        mt = at(R + 8192, 2, 2, 512)
        wo = at(HT, KD, D)
        x1 = at(R, NT, D)
        g1row = at(20480, 2, D)
        mt6 = at(22528, 2, 512)
        h2T = at(K, KD, T)
        slot = [at(4096 * i, 16, 256) for i in range(6)]
        M7 = 26520
        xeT = at(M7, KD, CAP)
        hid = at(M7 + 1280, KE, CAP)
        yT = at(M7 + 3840, KD, CAP)
        sil = at(M7 + 5120, 2, CAP)
        xg = at(M7 + 5440, 2, D)
        ye = at(M7 + 7488, 2, D)
        yf = at(0, NT, D)
        yo = at(10240, NT, D)
        fgb = at(R, D)

        C = R + 10240
        def const(*dims):
            nonlocal C
            v = at(C, *dims)
            C += int(np.prod(dims))
            return v
        ident, ones = const(P), const(P)
        colv = const(92)
        cs = const(KD, 2)
        modraw, mod = const(48, 2), const(48, 2)
        A1, A2 = const(KD, 2), const(KD, 2)
        dw = const(KC, TAPS)
        wr = const(KD, NE)
        ss, std, rstd = const(NT), const(NT), const(NT)
        eps = const(1)
        small = const(3, 16)
        marks = const(16)
        eps_zero = const(64)
        otok = const(2, P)
        mx, nmx, sums = const(2, 3), const(2), const(4, 2)
        rsum, rinv = const(4), const(4)
        lg, aff = const(NT, NE), const(NT, NE)
        gT, iT = const(2, NE), const(2, NE + 1)
        gidx, sidx = const(2), const(2)
        vals = const(CAP)
        idxu = const(CAP)
        idxf = const(CAP)
        rows, dwr = at(C, P), at(C + P, DC)
        braw = at(C, 2, SLOTS, GRID_W)
        mask = at(C + 2 * SLOTS * GRID_W, 10, GRID_W)
        diag = at(C, 2, P)
        affT = const(T)
        work = at(C, T)
        affT_scr = affT[:, 0:D]
        C += T
        assert C <= 53120, C
        CV = dict(c=0, ctx=8, n1=16, n2=24, bada=32, dwb=80, lng=84, lnb=88)
        sh1, sc1, g1c, sh2, sc2, g2c = (mod[:, 8 * i:8 * i + 8, :] for i in range(6))

        xhat = nc.dram_tensor("xhat", (T, D), F32, kind="Internal").ap()
        yacc = nc.dram_tensor("yacc", (T, D), F32, kind="Internal").ap()
        RP = 64
        NR = HEADS * RPB_R * RPB_C
        rpbp = nc.dram_tensor("rpbp", (RP + NR + RP,), F32, kind="Internal")
        rpbp_ap = rpbp.ap()

        w_in = A["w_in"][0].rearrange("(k p) n -> p k n", p=P)
        w_ada = A["w_ada"][0].rearrange("(k p) n -> p k n", p=P)
        w_pw = A["w_conv_pw"][0].rearrange("(k p) n -> p k n", p=P)
        w_ao = A["w_attn_o"][0].rearrange("(k p) n -> p k n", p=P)
        w_out = A["w_out"][0].rearrange("(k p) n -> p k n", p=P)
        w_g = A["w_gate_e"][0].rearrange("e (k p) n -> e p k n", p=P)
        w_u = A["w_up_e"][0].rearrange("e (k p) n -> e p k n", p=P)
        w_d = A["w_down_e"][0].rearrange("e (k p) n -> e p k n", p=P)

        rows_in, dwr_in, x_in, wr_in, mask_in = (sem(n) for n in ("rows_in", "dwr_in", "x_in", "wr_in", "mask_in"))
        kraw_in, vc_in, fg_in, wo_in = (sem(n) for n in ("kraw_in", "vc_in", "fg_in", "wo_in"))
        ws_in = [sem(f"ws_in{i}") for i in range(4)]
        wm_in = [sem(f"wm_in{i}") for i in range(2)]
        slot_in = [sem(f"slot_in{i}") for i in range(6)]
        bias_in, b14_ok = sem("bias_in"), sem("b14_ok")
        rpb_zero, rpb_done = sem("rpb_zero"), sem("rpb_done")
        idents = sem("idents")
        pre = sem("pre")
        colv_ok, cs_ok, dw_ok = sem("colv_ok"), sem("cs_ok"), sem("dw_ok")
        ada_ready, ada_copied = sem("ada_ready"), sem("ada_copied")
        mod1_ok, mod2_ok = sem("mod1_ok"), sem("mod2_ok")
        sq1, std1, xs1 = sem("sq1"), sem("std1"), sem("xs1")
        t1_ready, t1_act, t1_dve = sem("t1_ready"), sem("t1_act"), sem("t1_dve")
        pads, u_ready, sg_ok, u_free, qk_free = (sem(n) for n in ("pads", "u_ready", "sg_ok", "u_free", "qk_free"))
        v_ready, v_done = sem("v_ready"), sem("v_done")
        chain = sem("chain")
        conv_done = sem("conv_done")
        kc_ready, kc_done, ks_ready, ks_done = sem("kc_ready"), sem("kc_done"), sem("ks_ready"), sem("ks_done")
        ln_sum, ln_mid, ln_sq, ln_var, ln_std, ln_norm, ln_done = (
            sem(n) for n in ("ln_sum", "ln_mid", "ln_sq", "ln_var", "ln_std", "ln_norm", "ln_done"))
        bias_ok, qz_zero, qz_ok = sem("bias_ok"), sem("qz_zero"), sem("qz_ok")
        s_ready, s_added, nmax_ok, p_ok = sem("s_ready"), sem("s_added"), sem("nmax_ok"), sem("p_ok")
        tg_ready, tg_act, tg_dve, o_ready, o_done = sem("tg_ready"), sem("tg_act"), sem("tg_dve"), sem("o_ready"), sem("o_done")
        m_ready, m_sig, m_done = sem("m_ready"), sem("m_sig"), sem("m_done")
        g1_diag, g1_ps, g1_ok = sem("g1_diag"), sem("g1_ps"), sem("g1_ok")
        o6_ready, o6_done, x1_ok, sq6, std6, xs6 = (sem(n) for n in ("o6_ready", "o6_done", "x1_ok", "sq6", "std6", "xs6"))
        x_in6 = sem("x_in6")
        t6_ready, t6_act, t6_dve = sem("t6_ready"), sem("t6_act"), sem("t6_dve")
        lg_ready, ex_in, ex_ok, aff_ok, aT_ready, aT_ok, topk_ok, kt_ready, kt_ok = (
            sem(n) for n in ("lg_ready", "ex_in", "ex_ok", "aff_ok", "aT_ready", "aT_ok", "topk_ok", "kt_ready", "kt_ok"))
        yacc_out, xhat_out, state_out, y_out = sem("yacc_out"), sem("xhat_out"), sem("state_out"), sem("y_out")
        gidx_ok, gathered, tin_ready, xe_act, xe_dve = (sem(n) for n in ("gidx_ok", "gathered", "tin_ready", "xe_act", "xe_dve"))
        gu_ready, silu_ok, hid_ok, y_ready, yT_ok = (sem(n) for n in ("gu_ready", "silu_ok", "hid_ok", "y_ready", "yT_ok"))
        tb_ready, ye_ok, sidx_ok, scattered = sem("tb_ready"), sem("ye_ok"), sem("sidx_ok"), sem("scattered")
        sq8, std8, y_ok = sem("sq8"), sem("std8"), sem("y_ok")
        yf_in = [sem(f"yf_in{t}") for t in range(NT)]
        pe_turn, pool_turn = sem("pe_turn"), sem("pool_turn")
        m_free, vv_ready, e_loc, s_part, sum_ok, rinv_ok = (sem(n) for n in ("m_free", "vv_ready", "e_loc", "s_part", "sum_ok", "rinv_ok"))
        rinv6, router, q_ok = sem("rinv6"), sem("router"), sem("q_ok")

        UNITS = []
        for i, (r0, nr, sl) in enumerate(PAIRS):
            UNITS += [(i, r0 * GRID_W, nr, sl, hd) for hd in range(2)]
        for i in range(TP // P):
            UNITS += [(len(PAIRS) + i, TS, 0, 0, hd) for hd in range(2)]
        NU = len(UNITS)
        LOCAL_UNITS = 2 * len(PAIRS)

        def blocks(u):
            qt, tok, nr, _, _ = UNITS[u]
            if nr == 0:
                return [[(b * P, P, ("v", tok // P + b)) for b in range(TP // P)]]
            g = [[(b * P, P, ("v", tok // P + b)) for b in range(4)],
                 [(576 + b * P, P, ("c", b)) for b in range(4)]]
            if nr == 9:
                g.append([(512, GRID_W, ("v", tok // P + 4))])
            return g

        GROUPS = []

        def order():
            out = [("S", 0)]
            for u in range(NU):
                if u + 1 < NU:
                    out.append(("S", u + 1))
                if u >= 1:
                    out.append(("V", u - 1))
                out.append(("T", u))
                if u >= 3 and u % 2:
                    out.append(("O", (u - 3) // 2))
            out += [("V", NU - 1), ("O", NU // 2 - 1)]
            return out

        ORDER = order()
        for kind, n in ORDER:
            if kind == "T":
                GROUPS += [("P", n, g) for g in range(len(blocks(n)))]
            if kind == "O":
                GROUPS.append(("O", n, 0))
        NG = len(GROUPS)
        assert NG % 3 == 0, NG
        BY_DVE = [k == "P" and g == 0 for k, _, g in GROUPS]
        NG_DVE, NG_ACT = sum(BY_DVE), NG - sum(BY_DVE)

        def group_done_at(eng, hh, par, i):
            n = sum(x == BY_DVE[i] for x in BY_DVE[:i + 1])
            if BY_DVE[i]:
                eng.wait_ge(tg_dve, hh * (2 * NG_DVE) + (par * NG_DVE + n))
            else:
                eng.wait_ge(tg_act, hh * (2 * NG_ACT) + (par * NG_ACT + n))

        def groups_before(eng, hh, par):
            eng.wait_ge(tg_dve, hh * (2 * NG_DVE) + par * NG_DVE)
            eng.wait_ge(tg_act, hh * (2 * NG_ACT) + par * NG_ACT)

        block = ctx.enter_context(nc.Block())

        def tile_groups():
            return [(c, tc) for tc in range(3) for c in range(KD)]

        @block.sync
        def _(sp):
            def vec(name, row):
                n = int(np.prod(A[name].shape)) // P
                flat = A[name]
                while len(flat.shape) > 1:
                    flat = flat[0]
                sp.dma_start(rows[row:row + n, :], flat.rearrange("(k p) -> k p", p=P)).then_inc(rows_in, 16)
            for name, key in (("c", "c"), ("c_ctx", "ctx"), ("norm1_g", "n1"), ("norm2_g", "n2"), ("b_ada", "bada"),
                              ("conv_dw_b", "dwb"), ("conv_ln_g", "lng"), ("conv_ln_b", "lnb")):
                vec(name, CV[key])
            sp.dma_start(dwr[0:TAPS, :], A["conv_dw_w"][0]).then_inc(dwr_in, 16)

            def ws_load(s, src, n0, n1):
                sp.dma_start(ws[s][:, :, 0:P], src[:, :, ds(n0, P)]).then_inc(ws_in[s], 16)
                sp.dma_start(ws[s][:, :, P:2 * P], src[:, :, ds(n1, P)]).then_inc(ws_in[s], 16)

            for s in range(4):
                ws_load(s, w_ada, 256 * s, 256 * s + P)
            sp.dma_start(xin[:, 0:4, :], A["x_sample"][0, 0:512].rearrange("(t p) d -> p t d", p=P)).then_inc(x_in, 16)
            sp.dma_start(xin[:, 4:8, :], A["x_sample"][0, 512:1024].rearrange("(t p) d -> p t d", p=P)).then_inc(x_in, 16)
            sp.dma_start(xin[:, 8:10, :], A["x_prompt"][0].rearrange("(t p) d -> p t d", p=P)).then_inc(x_in, 16)
            for s in range(4):
                sp.wait_ge(ada_ready, s + 1)
                ws_load(s, w_ada, 1024 + 256 * s, 1024 + 256 * s + P)
            sp.dma_start(wr, A["w_router"][0].rearrange("(k p) n -> p k n", p=P)).then_inc(wr_in, 16)
            sp.wait_ge(rpb_zero, 1)
            sp.dma_start(rpbp_ap[0:RP].rearrange("(a b) -> a b", a=1), eps_zero[0:1, 0:RP]).then_inc(rpb_done, 16)
            sp.dma_start(rpbp_ap[RP + NR:].rearrange("(a b) -> a b", a=1), eps_zero[0:1, 0:RP]).then_inc(rpb_done, 16)
            sp.dma_start(rpbp_ap[RP:RP + NR].rearrange("(a b) -> a b", a=HEADS),
                         A["na_rpb"][0].rearrange("h r c -> h (r c)")).then_inc(rpb_done, 16)

            for half in range(2):
                with sp.Fori(0, 2) as i:
                    for jj in range(2):
                        if half == 0:
                            sp.wait_ge(ada_ready, 5 + jj)
                            sp.wait_ge(u_ready, i * (6 + 6 * jj))
                            ws_load(jj, w_in, i * 256 + P * jj, i * 256 + (DC + P * jj))
                        else:
                            sp.wait_ge(u_ready, i * 12 + (6 * jj + 18))
                            ws_load(jj, w_in, i * 256 + (1024 + P * jj), i * 256 + (1536 + P * jj))
                        for a in range(2):
                            n = 8 * half + 2 * jj + a
                            sp.wait_ge(ada_ready, i * 4 + (n + 7))
                            ws_load(2 + a, w_ada, i * 1024 + 256 * (8 + n), i * 1024 + (256 * (8 + n) + P))
            for jj in range(2):
                sp.wait_ge(u_ready, 6 * (7 + jj))
                ws_load(jj, w_in, 2048 + 256 * jj, 2048 + 256 * jj + P)
            sp.wait_ge(dw_ok, 1)
            sp.wait_ge(colv_ok, 1)
            sp.dma_start(mask, A["window_masks"]).then_inc(mask_in, 16)
            sp.wait_ge(v_ready, 20)
            sp.dma_start(vc, A["cache_ctx_v"][0, 0].rearrange("(t p) h d -> p t (h d)", p=P)).then_inc(vc_in, 16)
            sp.wait_ge(u_free, 15)
            sp.dma_start(kraw, A["cache_ctx_k"][0, 0].rearrange("(t p) h d -> p t (h d)", p=P)).then_inc(kraw_in, 16)
            sp.wait_ge(rpb_done, 48)
            sp.wait_ge(conv_done, 1)
            def load_bias(hp):
                for h in range(2):
                    for half in range(2):
                        off = RP + (1 - half) * RPB_C + 15 - (GRID_W - 1)
                        src = bass.AP(rpbp, off + (2 * hp + h) * RPB_R * RPB_C,
                                      [[1, GRID_W], [RPB_C, SLOTS], [1, GRID_W]])
                        sp.dma_start(braw[64 * half:64 * half + 64, h, :, :], src).then_inc(bias_in, 16)
            for hp in range(4):
                if hp == 1:
                    sp.wait_ge(ks_done, 2)
                    sp.dma_start(O["state_k"][0, 0].rearrange("(t p) h d -> p t (h d)", p=P), kst).then_inc(state_out, 16)
                    sp.wait_ge(v_done, 20)
                    sp.dma_start(O["state_v"][0, 0].rearrange("(t p) h d -> p t (h d)", p=P), vtok[:, 8:10, :]).then_inc(state_out, 16)
                if hp:
                    sp.wait_ge(b14_ok, 2 * hp)
                load_bias(hp)
            sp.wait_ge(o_done, 4 * NU // 2)
            sp.wait_ge(tg_act, 4 * NG_ACT)
            sp.wait_ge(tg_dve, 4 * NG_DVE)
            sp.wait_ge(state_out, 32)

            def wm_load(s, n0):
                for k0, nk, src in ((0, 8, w_in[:, :, ds(n0 + 2560, P)]), (8, 8, w_in[:, :, ds(n0 + 3584, P)]),
                                    (16, 4, w_pw[:, :, ds(n0, P)]), (20, 4, w_ao[:, :, ds(n0, P)])):
                    sp.dma_start(wm[s][:, k0:k0 + nk, :], src).then_inc(wm_in[s], 16)
            sp.wait_ge(vv_ready, 4 * NU)
            wm_load(0, 0)
            wm_load(1, P)
            with sp.Fori(0, 3) as i:
                for s in range(2):
                    sp.wait_ge(m_ready, i * 6 + 3 * (s + 1))
                    wm_load(s, i * 256 + (256 + P * s))
            sp.wait_ge(m_ready, 24)
            sp.dma_start(wo, w_out).then_inc(wo_in, 16)
            sp.wait_ge(m_done, 24)
            sp.dma_start(x1[:, 0:8, :], A["x_sample"][0].rearrange("(t p) d -> p t d", p=P)).then_inc(x_in6, 16)
            sp.dma_start(x1[:, 8:10, :], A["x_prompt"][0].rearrange("(t p) d -> p t d", p=P)).then_inc(x_in6, 16)

            def expert_load(e, c):
                s = (c + 2) % 6
                if c < 8:
                    sp.dma_start(slot[s][:, 0:8, :], w_g[e, :, :, 256 * c:256 * c + 256]).then_inc(slot_in[s], 16)
                    sp.dma_start(slot[s][:, 8:16, :], w_u[e, :, :, 256 * c:256 * c + 256]).then_inc(slot_in[s], 16)
                else:
                    n = 256 * (c - 8)
                    sp.dma_start(slot[s][:, 8:16, :], w_d[e, :, 8:16, n:n + 256]).then_inc(slot_in[s], 16)
                    sp.dma_start(slot[s][:, 0:8, :], w_d[e, :, 0:8, n:n + 256]).then_inc(slot_in[s], 16)
            for c in range(3):
                expert_load(0, c)
            for t in range(NT):
                sp.wait_ge(x1_ok, 2 * t + 2)
                sp.dma_start(yacc[P * t:P * t + P, :], x1[:, t, :]).then_inc(yacc_out, 16)
            expert_load(0, 3)
            expert_load(0, 4)
            expert_load(0, 5)
            for t in range(NT):
                sp.wait_ge(xs6, t + 1)
                sp.dma_start(xhat[P * t:P * t + P, :], x1[:, t, :]).then_inc(xhat_out, 16)
            sp.wait_ge(t6_ready, 24)
            sp.wait_ge(xhat_out, 16 * NT)
            sp.dma_start(fgb, A["final_g"].partition_broadcast(P)).then_inc(fg_in, 16)

            def second_half(e):
                for c in range(6, 12):
                    sp.wait_ge(gu_ready, e * 16 + 2 * (c - 5))
                    expert_load(e, c)
            with sp.Fori(0, NE - 1) as e:
                second_half(e)
                for c in range(6):
                    if c < 2:
                        sp.wait_ge(gu_ready, e * 16 + 2 * (c + 7))
                    else:
                        sp.wait_ge(y_ready, e * 8 + 2 * (c - 1))
                    expert_load(e + 1, c)
            second_half(NE - 1)
            sp.wait_ge(scattered, 32 * NE)
            sp.wait_ge(y_ready, 8 * NE)
            for t in range(NT):
                sp.dma_start(yf[:, t, :], yacc[P * t:P * t + P, :]).then_inc(yf_in[t], 16)
            for t in range(NT):
                dst = O["y_sample"][0, P * t:P * t + P, :] if t < TS // P else O["y_prompt"][0, P * t - TS:P * t - TS + P, :]
                sp.wait_ge(y_ok, t + 1)
                sp.dma_start(dst, yo[:, t, :]).then_inc(y_out, 16)
            sp.wait_ge(y_out, 16 * NT)
            sp.wait_ge(yacc_out, 16 * NT)

        @block.gpsimd
        def _(pool):
            nc.gpsimd.memset(ident, 0.0).then_inc(idents, 1)
            nc.gpsimd.memset(ones, 1.0).then_inc(idents, 1)
            nc.gpsimd.memset(eps, EPS).then_inc(idents, 1)
            pool.wait_ge(idents, 3)
            nc.gpsimd.affine_select(out=ident, in_=ident, compare_op=ALU.not_equal, fill=1.0, base=0,
                                    pattern=[[-1, P]], channel_multiplier=1).then_inc(idents, 1)
            nc.gpsimd.memset(eps_zero[0:1, :], 0.0).then_inc(rpb_zero, 1)
            nc.gpsimd.memset(glu, 0.0).then_inc(pads, 1)
            pool.wait_ge(ln_done, 3)
            pool.wait_ge(v_ready, 20)
            nc.gpsimd.memset(qz, 0.0).then_inc(qz_zero, 1)
            pool.wait_ge(qz_zero, 1)
            pool.wait_ge(qk_free, 15)
            pool.wait_ge(mask_in, 16)
            with pool.Fori(0, 2) as hh:
                for par in range(2):
                    pool.wait_ge(bias_in, hh * 128 + (64 * par + 64))
                    pool.wait_ge(qz_ok, hh * (2 * NU) + par * NU)
                    for h in range(2):
                        m = mask[:, 0:1, :].to_broadcast((P, SLOTS, GRID_W))
                        nc.gpsimd.tensor_tensor(bias[par][h][0], braw[:, h, :, ::-1], m, ALU.add).then_inc(b14_ok, 1)
                    pool.wait_ge(b14_ok, hh * 4 + (2 * par + 2))
                    for h in range(2):
                        b14, b9 = bias[par][h]
                        nc.gpsimd.tensor_tensor(b9, b14[:, 2:11, :], mask[:, 1:10, :], ALU.add).then_inc(bias_ok, 1)
                    for u in range(NU):
                        qt, _, _, _, hd = UNITS[u]
                        if par or u >= 4:
                            pool.wait_ge(s_ready, hh * (2 * NU) + (par * NU + u - 3))
                        else:
                            pool.wait_ge(s_ready, hh * (2 * NU))
                        if u == 0:
                            pool.wait_ge(bias_ok, hh * 4 + (2 * par + 2))
                        pool.wait_ge(qz_ok, hh * (2 * NU) + (par * NU + u))
                        half = slice(64 * hd, 64 * hd + 64)
                        nc.gpsimd.tensor_copy(qz[half, u % 4, :],
                                              qT[half, ds(hh * 2 + par, 1), qt * P:qt * P + P].rearrange("p a n -> p (a n)")).then_inc(qz_ok, 1)
            pool.wait_ge(xhat_out, 16 * NT)
            pool.wait_ge(yacc_out, 16 * NT)

            def gather(e):
                pool.wait_ge(gidx_ok, e + 1)
                pool.wait_ge(tin_ready, e * 16)
                pool.sem_inc(pool_turn, 1)
                for i, cap in enumerate((CAP_S, CAP_P)):
                    nc.gpsimd.indirect_dma_start(
                        out=xg[0:cap, i, :], out_offset=None, in_=xhat,
                        in_offset=bass.IndirectOffsetOnAxis(ap=gidx[0:cap, i:i + 1].bitcast(U32), axis=0)).then_inc(gathered, 16)
            gather(0)
            with pool.Fori(0, NE) as e:
                gather(e + 1)
                pool.wait_ge(ye_ok, e * 4 + 4)
                pool.wait_ge(sidx_ok, e + 1)
                pool.wait_ge(scattered, e * 32)
                pool.sem_inc(pool_turn, 1)
                for i, cap in enumerate((CAP_S, CAP_P)):
                    nc.gpsimd.indirect_dma_start(
                        out=yacc, out_offset=bass.IndirectOffsetOnAxis(ap=sidx[0:cap, i:i + 1].bitcast(U32), axis=0),
                        in_=ye[0:cap, i, :], in_offset=None, compute_op=ALU.add).then_inc(scattered, 16)
            pool.wait_ge(gathered, 32 * (NE + 1))
            pool.wait_ge(scattered, 32 * NE)

        @block.tensor
        def _(pe):
            def mm(out, lhsT, rhs, start, stop):
                return nc.tensor.matmul(out, lhsT, rhs, start=start, stop=stop)

            def tr(out, in_, n):
                return nc.tensor.transpose(out, in_, ident[0:n, 0:n])

            pe.wait_ge(idents, 4)
            pe.wait_ge(rows_in, 16 * 8)
            tr(bank[4][:, 0:92], rows[0:92, :], 92).then_inc(pre, 1)
            pe.wait_ge(dwr_in, 16)
            for k in range(KC):
                last = tr(bank[5][:, 32 * k:32 * k + TAPS], dwr[0:TAPS, P * k:P * k + P], TAPS)
            last.then_inc(pre, 1)
            pe.wait_ge(cs_ok, 2)

            def ada(s, b):
                for half in range(2):
                    for k in range(KD):
                        last = mm(bank[b][:, 2 * half:2 * half + 2], ws[s][:, k, P * half:P * half + P], cs[:, k, :],
                                  k == 0, k == KD - 1)
                last.then_inc(ada_ready, 1)

            with pe.Fori(0, 2) as i:
                for s in range(4):
                    pe.wait_ge(ws_in[s], i * 32 + 32)
                    pe.wait_ge(ada_copied, i * 4 + (s + 1))
                    ada(s, 6 + s % 2)

            def turn(src, scaled, ready, act_done, dve_done, step):
                for g, (c, tc) in enumerate(tile_groups()):
                    t0, n = TOK[tc]
                    if c == 0:
                        pe.wait_ge(scaled, (t0 + n) // P)
                    if g >= 4:
                        pe.wait_ge(dve_done if g % 2 else act_done, (g - 4) // 2 + 1)
                    for t in range(n // P):
                        last = tr(bank[g % 4][:, P * t:P * t + P], src[:, t0 // P + t, P * c:P * c + P], P)
                    last.then_inc(ready, 1)
            turn(xin, xs1, t1_ready, t1_act, t1_dve, 0)
            pe.wait_ge(t1_act, 12)
            pe.wait_ge(t1_dve, 12)

            for half in range(2):
                if half:
                    pe.wait_ge(u_free, 15)
                with pe.Fori(0, 2) as i:
                    for jj in range(2):
                        pe.wait_ge(ws_in[jj], i * 32 + (96 + 64 * half))
                        for tc, (t0, n) in enumerate(TOK):
                            pe.wait_ge(qk_free if half else u_free, i * 6 + (3 * jj + tc + 1))
                            for h in range(2):
                                for k in range(KD):
                                    last = mm(bank[2 * tc + h][:, 0:n], ws[jj][:, k, P * h:P * h + P], hT[:, k, t0:t0 + n],
                                              k == 0, k == KD - 1)
                                last.then_inc(u_ready, 1)
                        for a in range(2):
                            pe.wait_ge(ws_in[2 + a], i * 64 + (128 * half + 32 * jj + 96))
                            pe.wait_ge(ada_copied, i * 4 + (8 * half + 2 * jj + a + 9))
                            ada(2 + a, 6 + a)
            for n in range(20):
                jj, t = divmod(n, NT)
                if t == 0:
                    pe.wait_ge(ws_in[jj], 32 * 7)
                if n < 6:
                    pe.wait_ge(qk_free, 15)
                else:
                    pe.wait_ge(v_done, n - 5)
                for k in range(KD):
                    last = mm(bank[n % 6][:, 0:256], hT[:, k, P * t:P * t + P], ws[jj][:, k, :], k == 0, k == KD - 1)
                last.then_inc(v_ready, 1)
            pe.wait_ge(v_done, 20)
            for t in range(2):
                for h in range(KC):
                    last = tr(bank[4 + t][:, P * h:P * h + P], kT[:, h, TS + P * t:TS + P * t + P], P)
                last.then_inc(ks_ready, 1)

            pe.wait_ge(conv_done, 1)
            for tc, (t0, n) in enumerate(TOK):
                c0 = CONV_AT[tc]
                for k in range(KC):
                    last = mm(bank[0][:, 0:n], ones, conv[:, k, c0:c0 + n], k == 0, k == KC - 1)
                last.then_inc(ln_sum, 1)
                pe.wait_ge(ln_sq, tc + 1)
                for k in range(KC):
                    last = mm(bank[1][:, 0:n], ones, sq[:, k, 0:n], k == 0, k == KC - 1)
                last.then_inc(ln_var, 1)

            pe.wait_ge(kraw_in, 16)
            pe.wait_ge(ln_std, 3)
            for h in range(KC):
                for t in range(PAST // P):
                    last = tr(bank[h][:, P * t:P * t + P], kraw[:, t, P * h:P * h + P], P)
                last.then_inc(kc_ready, 1)
            pe.wait_ge(kc_done, 4)
            pe.wait_ge(ks_done, 2)
            pe.wait_ge(vc_in, 16)

            SL, SC, TB, OB = (0, 1), (2, 3), (4, 5, 6), 7

            def head_pair(t, tile_of, hp):
                return t[:, ds(hp, 1), tile_of].rearrange("p a n -> p (a n)")

            with pe.Fori(0, 2) as hh:
                for par in range(2):
                    hp = hh * 2 + par
                    su = hh * (2 * NU) + par * NU
                    sl_ = hh * (2 * LOCAL_UNITS) + par * LOCAL_UNITS
                    gcount = 0
                    for kind, u in ORDER:
                        qt, tok, nr, _, hd = UNITS[min(u, NU - 1)]
                        if kind == "S":
                            pe.wait_ge(qz_ok, su + (u + 1))
                            if u >= 2:
                                pe.wait_ge(p_ok, su + (u - 1))
                            if nr:
                                if u >= 1:
                                    pe.wait_ge(s_added, sl_ + u)
                                w = nr * GRID_W // 2
                                for b in range(2):
                                    mm(bank[SL[b]][:, 0:w], qz[:, u % 4, :], head_pair(kT, slice(tok + b * w, tok + b * w + w), hp), True, True)
                                last = mm(bank[SC[u % 2]][:, 0:PAST], qz[:, u % 4, :], head_pair(kcT, slice(0, PAST), hp), True, True)
                            else:
                                last = mm(bank[SC[u % 2]][:, 0:TP], qz[:, u % 4, :], head_pair(kT, slice(TS, T), hp), True, True)
                            last.then_inc(s_ready, 1)
                        if kind == "T":
                            pe.wait_ge(p_ok, su + (u + 1))
                            for g in blocks(u):
                                if gcount >= 3:
                                    group_done_at(pe, hh, par, gcount - 3)
                                elif gcount == 0:
                                    groups_before(pe, hh, par)
                                if g[0][1] < P:
                                    pe.sem_inc(pe_turn, 1)
                                for b, (col, n, _) in enumerate(g):
                                    last = tr(bank[TB[gcount % 3]][0:n, P * b:P * b + P], Pr[:, u % 2, col:col + n], P)
                                last.then_inc(tg_ready, 1)
                                gcount += 1
                        if kind == "V":
                            g0 = GROUPS.index(("P", u, 0))
                            flat = [(i, b, blk) for i, g in enumerate(blocks(u)) for b, blk in enumerate(g)]
                            if hd == 0:
                                pe.wait_ge(o_done, hh * NU + (par * NU // 2 + u // 2))
                            seen = -1
                            for m, (i, b, (col, n, (src, st))) in enumerate(flat):
                                if i != seen:
                                    group_done_at(pe, hh, par, g0 + i)
                                    seen = i
                                vsrc = vc if src == "c" else vtok
                                last = mm(bank[OB][:, DH * hd:DH * hd + DH], PT[0:n, u % 2, P * (4 * i + b):P * (4 * i + b) + P],
                                          vsrc[0:n, st, ds(hp * P + DH * hd, DH)], m == 0, m == len(flat) - 1)
                            last.then_inc(vv_ready, 1)
                        if kind == "O":
                            pe.wait_ge(o_done, hh * NU + (par * NU // 2 + u + 1))
                            group_done_at(pe, hh, par, gcount - 3)
                            tr(bank[TB[gcount % 3]][:, 0:P], otok[:, u % 2, :], P).then_inc(tg_ready, 1)
                            gcount += 1

            pe.wait_ge(tg_act, 4 * NG_ACT)
            pe.wait_ge(tg_dve, 4 * NG_DVE)
            with pe.Fori(0, 4) as i:
                for s in range(2):
                    pe.wait_ge(wm_in[s], i * 64 + 64)
                    for tc, (t0, n) in enumerate(TOK):
                        b = 4 * ((3 * s + tc) % 2)
                        pe.wait_ge(m_free, i * 6 + (3 * s + tc + 1))
                        for which, k0, nk, src, c0 in ((0, 0, 8, hT, t0), (1, 8, 8, hT, t0), (2, 16, 4, conv, CONV_AT[tc]), (3, 20, 4, qT, t0)):
                            for k in range(nk):
                                last = mm(bank[b + which][:, 0:n], wm[s][:, k0 + k, :], src[:, k, c0:c0 + n], k == 0, k == nk - 1)
                        last.then_inc(m_ready, 1)

            for cnd in range(2):
                for c in range(KD):
                    n = cnd * KD + c
                    pe.wait_ge(g1_diag, n + 1)
                    if c == 0:
                        pe.wait_ge(m_done, 24)
                    last = mm(bank[4 + 2 * cnd + c // 4][:, P * (c % 4):P * (c % 4) + P], ones, diag[:, n % 2, :], True, True)
                    last.then_inc(g1_ps, 1)
            pe.wait_ge(wo_in, 16)
            for t in range(NT):
                for h in range(2):
                    n = 2 * t + h
                    if n >= 4:
                        pe.wait_ge(o6_done, n - 3)
                    for k in range(KD):
                        last = mm(bank[n % 4][:, :], merged[:, k, P * t:P * t + P], wo[:, k, 512 * h:512 * h + 512], k == 0, k == KD - 1)
                    last.then_inc(o6_ready, 1)
            pe.wait_ge(o6_done, 20)
            turn(x1, xs6, t6_ready, t6_act, t6_dve, 1)
            pe.wait_ge(wr_in, 16)
            pe.wait_ge(t6_act, 12)
            pe.wait_ge(t6_dve, 12)
            for t in range(NT):
                for k in range(KD):
                    last = mm(bank[4][:, NE * t:NE * t + NE], h2T[:, k, P * t:P * t + P], wr[:, k, :], k == 0, k == KD - 1)
            last.then_inc(lg_ready, 1)
            pe.wait_ge(aff_ok, 1)
            for t in range(NT):
                last = tr(bank[t // 4][0:NE, P * (t % 4):P * (t % 4) + P], aff[:, t, :], P)
            last.then_inc(aT_ready, 1)
            pe.wait_ge(topk_ok, 1)
            tr(bank[5][:, 0:NE], vals[0:NE, 0:CAP_S], NE)
            tr(bank[5][0:CAP_P, NE:2 * NE], vals[0:NE, CAP_S:CAP], NE)
            tr(bank[5][:, 2 * NE:3 * NE], idxf[0:NE, 0:CAP_S], NE)
            tr(bank[5][0:CAP_P, 3 * NE:4 * NE], idxf[0:NE, CAP_S:CAP], NE).then_inc(kt_ready, 1)

            def gathered_in(e, before):
                pe.wait_ge(gathered, 32 * e + 32)
                pe.wait_ge(ye_ok, before * 4)
                for c in range(KD):
                    tr(bank[4 + c // 4][:, P * (c % 4):P * (c % 4) + P], xg[:, 0, P * c:P * c + P], P).then_inc(tin_ready, 1)
                for c in range(KD):
                    tr(bank[6][:, CAP_P * c:CAP_P * c + CAP_P], xg[0:CAP_P, 1, P * c:P * c + P], CAP_P).then_inc(tin_ready, 1)

            pe.wait_ge(kt_ok, 1)
            gathered_in(0, 0)
            with pe.Fori(0, NE) as e:
                pe.wait_ge(xe_act, e * 8 + 8)
                pe.wait_ge(xe_dve, e * 8 + 8)
                for c in range(8):
                    s = (c + 2) % 6
                    pe.wait_ge(slot_in[s], e * 64 + 32 * (c // 6 + 1))
                    for ff in range(2):
                        f = 2 * c + ff
                        if f >= 2:
                            pe.wait_ge(hid_ok, e * 16 + (f - 1))
                        for half in range(2):
                            for k in range(KD):
                                last = mm(bank[f % 2][:, CAP * half:CAP * half + CAP], slot[s][:, 8 * half + k, P * ff:P * ff + P],
                                          xeT[:, k, :], k == 0, k == KD - 1)
                        last.then_inc(gu_ready, 1)
                gathered_in(e + 1, e)
                pe.wait_ge(hid_ok, e * 16 + 16)
                for c in range(8, 12):
                    s = (c + 2) % 6
                    pe.wait_ge(slot_in[s], e * 64 + 64)
                    for dd in range(2):
                        d = 2 * (c - 8) + dd
                        if d >= 2:
                            pe.wait_ge(yT_ok, e * 8 + (d - 1))
                        for f in range(KE):
                            last = mm(bank[2 + d % 2][:, 0:CAP], slot[s][:, f, P * dd:P * dd + P], hid[:, f, :], f == 0, f == KE - 1)
                        last.then_inc(y_ready, 1)
                pe.wait_ge(xe_act, e * 8 + 16)
                pe.wait_ge(xe_dve, e * 8 + 16)
                for d in range(KD):
                    pe.wait_ge(yT_ok, e * 8 + (d + 1))
                    tr(bank[4 + d // 4][:, P * (d % 4):P * (d % 4) + P], yT[:, d, 0:CAP_S], P)
                    last = tr(bank[6 + d // 4][0:CAP_P, P * (d % 4):P * (d % 4) + P], yT[:, d, CAP_S:CAP], P)
                    if d % 4 == 3:
                        last.then_inc(tb_ready, 1)

        @block.scalar
        def _(act):
            A_ = nc.scalar.activation
            act.wait_ge(colv_ok, 1)
            A_(cs[:, :, 0], colv[:, 0:KD], ACT.Silu).then_inc(cs_ok, 1)
            A_(cs[:, :, 1], colv[:, KD:2 * KD], ACT.Silu).then_inc(cs_ok, 1)

            def ada_copy(b, n, tile0):
                act.wait_ge(ada_ready, n)
                A_(modraw[:, ds(tile0, 2), :], bank[b][:, 0:4].rearrange("p (a c) -> p a c", c=2), ACT.Copy).then_inc(ada_copied, 1)

            act.wait_ge(u_free, 3)
            with act.Fori(0, 2) as i:
                for s in range(4):
                    ada_copy(6 + s % 2, i * 4 + (s + 1), i * 8 + 2 * s)

            def x_arrived(t):
                if t in (0, 4, 8):
                    act.wait_ge(x_in, 48)
            for t in range(NT):
                x_arrived(t)
                if t:
                    act.wait_ge(sq1, t)
                A_(arena[:, R + 8192:R + 8192 + D], xin[:, t, :], ACT.Square, accum_out=ss[:, t:t + 1]).then_inc(sq1, 1)
            act.wait_ge(sq1, NT)
            A_(std, ss, ACT.Sqrt, bias=eps, scale=1.0 / D).then_inc(std1, 1)

            def leave(dst, Ac, Bc, ready, done):
                for g, (c, tc) in enumerate(tile_groups()):
                    if g % 2 == 0:
                        t0, n = TOK[tc]
                        cnd = 1 if tc == 2 else 0
                        act.wait_ge(ready, g + 1)
                        A_(dst[:, c, t0:t0 + n], bank[g % 4][:, 0:n], ACT.Identity, bias=Bc[:, c, cnd:cnd + 1],
                           scale=Ac[:, c, cnd:cnd + 1]).then_inc(done, 1)
            act.wait_ge(mod1_ok, 1)
            leave(hT, A1, sh1, t1_ready, t1_act)

            with act.Fori(0, 2) as i:
                for jj in range(2):
                    for tc, (t0, n) in enumerate(TOK):
                        m = 3 * jj + tc
                        act.wait_ge(u_ready, i * 12 + 2 * (m + 1))
                        act.wait_ge(u_free, i * 6 + (m + 2))
                        A_(sg[:, m % 2, 0:n], bank[2 * tc + 1][:, 0:n], ACT.Sigmoid).then_inc(sg_ok, 1)
                    for a in range(2):
                        ada_copy(6 + a, i * 4 + (2 * jj + a + 9), i * 8 + (16 + 4 * jj + 2 * a))
            with act.Fori(0, 2) as i:
                for jj in range(2):
                    for tc, (t0, n) in enumerate(TOK):
                        m = 3 * jj + tc
                        act.wait_ge(u_ready, i * 12 + (24 + 2 * (m + 1)))
                        A_(qT[:, ds(i * 2 + jj, 1), t0:t0 + n].rearrange("p a n -> p (a n)"), bank[2 * tc][:, 0:n], ACT.Copy, scale=DH ** -0.5).then_inc(q_ok, 1)
                        A_(kT[:, ds(i * 2 + jj, 1), t0:t0 + n].rearrange("p a n -> p (a n)"), bank[2 * tc + 1][:, 0:n], ACT.Copy).then_inc(qk_free, 1)
                    for a in range(2):
                        ada_copy(6 + a, i * 4 + (2 * jj + a + 17), i * 8 + (32 + 4 * jj + 2 * a))
            for n in range(20):
                jj, t = divmod(n, NT)
                act.wait_ge(v_ready, n + 1)
                A_(vtok[:, t, 256 * jj:256 * jj + 256], bank[n % 6][:, 0:256], ACT.Copy).then_inc(v_done, 1)

            for tc, (t0, n) in enumerate(TOK):
                c0 = CONV_AT[tc]
                act.wait_ge(ln_mid, 4 * (tc + 1))
                act.wait_ge(v_ready, 20)
                A_(sq[:, :, 0:n], conv[:, :, c0:c0 + n], ACT.Square).then_inc(ln_sq, 1)
                act.wait_ge(ln_var, tc + 1)
                A_(rs[:, 0:n], bank[1][:, 0:n], ACT.Sqrt, bias=eps, scale=1.0 / DC).then_inc(ln_std, 1)
                for k in range(KC):
                    act.wait_ge(ln_norm, 4 * tc + k + 1)
                    last = A_(conv[:, k, c0:c0 + n], conv[:, k, c0:c0 + n], ACT.Silu, scale=colv[:, CV["lng"] + k:CV["lng"] + k + 1],
                              bias=colv[:, CV["lnb"] + k:CV["lnb"] + k + 1])
                last.then_inc(ln_done, 1)
            for t in range(2):
                act.wait_ge(ks_ready, t + 1)
                A_(kst[:, t, :], bank[4 + t][:, :], ACT.Copy).then_inc(ks_done, 1)
            for h in range(KC):
                act.wait_ge(kc_ready, h + 1)
                A_(kcT[:, h, :], bank[h][:, :], ACT.Copy).then_inc(kc_done, 1)

            act.wait_ge(state_out, 32)
            SC, TB = (2, 3), (4, 5, 6)
            plan = []
            for kind, n in ORDER:
                if kind == "S" and n >= 0:
                    plan.append(("E", n))
                if kind == "T":
                    plan += [("G", GROUPS.index(("P", n, g))) for g in range(len(blocks(n)))]
                if kind == "O":
                    plan.append(("G", GROUPS.index(("O", n, 0))))
            with act.Fori(0, 2) as hh:
                for par in range(2):
                    hp = hh * 2 + par
                    su = hh * (2 * NU) + par * NU
                    for kind, n in plan:
                        if kind == "E":
                            u = n
                            nr = UNITS[u][2]
                            act.wait_ge(nmax_ok, su + (u + 1))
                            gprev = GROUPS.index(("P", u - 2, len(blocks(u - 2)) - 1)) + 1 if u >= 2 else 0
                            if u >= 4:
                                act.wait_ge(sum_ok, su + (u - 3))
                            act.wait_ge(tg_ready, hh * (2 * NG) + (par * NG + gprev))
                            if nr:
                                act.wait_ge(s_added, hh * (2 * LOCAL_UNITS) + (par * LOCAL_UNITS + u + 1))
                                A_(Pr[:, u % 2, 0:nr * GRID_W], S[:, u % 2, 0:nr * GRID_W], ACT.Exp, bias=nmx[:, u % 2:u % 2 + 1],
                                   accum_out=sums[:, u % 4, 0:1]).then_inc(e_loc, 1)
                                A_(Pr[:, u % 2, 576:576 + PAST], bank[SC[u % 2]][:, 0:PAST], ACT.Exp, bias=nmx[:, u % 2:u % 2 + 1],
                                   accum_out=sums[:, u % 4, 1:2]).then_inc(p_ok, 1)
                            else:
                                A_(Pr[:, u % 2, 0:TP], bank[SC[u % 2]][:, 0:TP], ACT.Exp, bias=nmx[:, u % 2:u % 2 + 1],
                                   accum_out=sums[:, u % 4, 1:2]).then_inc(p_ok, 1)
                        elif not BY_DVE[n]:
                            what, m, g = GROUPS[n]
                            act.wait_ge(tg_ready, hh * (2 * NG) + (par * NG + n + 1))
                            src = bank[TB[n % 3]]
                            if what == "O":
                                A_(qT[:, ds(hp, 1), P * m:P * m + P].rearrange("p a n -> p (a n)"), src[:, 0:P], ACT.Copy).then_inc(tg_act, 1)
                            else:
                                if m >= 2:
                                    act.wait_ge(vv_ready, su + (m - 1))
                                blk = blocks(m)[g]
                                A_(PT[0:blk[0][1], m % 2, 512 * g:512 * g + P * len(blk)], src[0:blk[0][1], 0:P * len(blk)], ACT.Copy).then_inc(tg_act, 1)

            with act.Fori(0, 4) as i:
                for s in range(2):
                    for tc, (t0, n) in enumerate(TOK):
                        m = 3 * s + tc
                        act.wait_ge(m_ready, i * 6 + (m + 1))
                        act.wait_ge(m_free, i * 6 + (m + 1))
                        for g in range(2):
                            last = A_(gs[:, m % 2, g, 0:n], bank[4 * (m % 2) + g][:, 0:n], ACT.Sigmoid)
                            last.then_inc(m_sig, 1)
            for cnd in range(2):
                for h in range(2):
                    act.wait_ge(g1_ps, 8 * cnd + 4 * h + 4)
                    A_(g1row[:, cnd, 512 * h:512 * h + 512], bank[4 + 2 * cnd + h][:, :], ACT.Copy).then_inc(g1_ok, 1)
            for t in range(NT):
                act.wait_ge(x1_ok, 2 * t + 2)
                if t:
                    act.wait_ge(sq6, t)
                A_(affT_scr, x1[:, t, :], ACT.Square, accum_out=ss[:, t:t + 1]).then_inc(sq6, 1)
            act.wait_ge(sq6, NT)
            A_(std, ss, ACT.Sqrt, bias=eps, scale=1.0 / D).then_inc(std6, 1)
            leave(h2T, A2, sh2, t6_ready, t6_act)
            act.wait_ge(ex_in, 1)
            A_(aff, lg, ACT.Exp).then_inc(ex_ok, 1)
            for b in range(3):
                act.wait_ge(aT_ready, 1)
                w = min(512, T - 512 * b)
                A_(affT[0:NE, 512 * b:512 * b + w], bank[b][0:NE, 0:w], ACT.Copy).then_inc(aT_ok, 1)

            def xe_leave(e):
                for c in range(KD):
                    act.wait_ge(tin_ready, e * 16 + (8 if c >= 0 else 0))
                    A_(xeT[:, c, 0:CAP_S], bank[4 + c // 4][:, P * (c % 4):P * (c % 4) + P], ACT.Identity,
                       bias=sh2[:, c, 0:1], scale=A2[:, c, 0:1]).then_inc(xe_act, 1)
            xe_leave(0)
            with act.Fori(0, NE) as e:
                for f in range(KE):
                    act.wait_ge(gu_ready, e * 16 + (f + 1))
                    if f >= 2:
                        act.wait_ge(hid_ok, e * 16 + (f - 1))
                    A_(sil[:, f % 2, :], bank[f % 2][:, 0:CAP], ACT.Silu).then_inc(silu_ok, 1)
                xe_leave(e + 1)
                for d in range(KD):
                    act.wait_ge(y_ready, e * 8 + (d + 1))
                    A_(yT[:, d, 0:CAP_S], bank[2 + d % 2][:, 0:CAP_S], ACT.Copy, scale=g2c[:, d, 0:1])
                    A_(yT[:, d, CAP_S:CAP], bank[2 + d % 2][:, CAP_S:CAP], ACT.Copy, scale=g2c[:, d, 1:2]).then_inc(yT_ok, 1)
            for t in range(NT):
                act.wait_ge(yf_in[t], 16)
                if t:
                    act.wait_ge(sq8, t)
                A_(affT_scr, yf[:, t, :], ACT.Square, accum_out=ss[:, t:t + 1]).then_inc(sq8, 1)
            act.wait_ge(sq8, NT)
            A_(std, ss, ACT.Sqrt, bias=eps, scale=1.0 / D).then_inc(std8, 1)

        @block.vector
        def _(dve):
            V_ = nc.vector
            steps = [0]

            def link(ins):
                steps[0] += 1
                ins.then_inc(chain, 1)
                dve.wait_ge(chain, steps[0])

            V_.memset(marks[:, 0:1], 0.0).then_inc(ada_copied, 2)
            V_.memset(marks[:, 1:2], 0.0).then_inc(u_free, 3)
            V_.memset(marks[:, 2:3], 0.0).then_inc(m_free, 2)
            V_.memset(marks[:, 8:9], 0.0).then_inc(qk_free, 3)
            dve.wait_ge(pre, 1)
            V_.tensor_copy(colv, bank[4][:, 0:92]).then_inc(colv_ok, 1)
            dve.wait_ge(pre, 2)
            V_.tensor_copy(dw, bank[5][:, 0:P].rearrange("p (k t) -> p k t", t=32)[:, :, 0:TAPS]).then_inc(dw_ok, 1)
            dve.wait_ge(colv_ok, 1)

            def bcast(col, n):
                return colv[:, col:col + n].unsqueeze(2).to_broadcast((P, n, 2))
            dve.wait_ge(ada_copied, 10)
            link(V_.tensor_tensor(mod[:, 0:16, :], modraw[:, 0:16, :], bcast(CV["bada"], 16), ALU.add))
            link(V_.scalar_tensor_tensor(out=A1, in0=sc1, scalar=1.0, in1=bcast(CV["n1"], KD), op0=ALU.add, op1=ALU.mult))
            V_.memset(marks[:, 3:4], 0.0).then_inc(mod1_ok, 1)
            dve.wait_ge(std1, 1)
            link(V_.reciprocal(rstd, std))
            for t in range(NT):
                V_.tensor_scalar(xin[:, t, :], xin[:, t, :], rstd[:, t:t + 1], None, ALU.mult).then_inc(xs1, 1)

            def leave(dst, Ac, Bc, ready, done):
                for g, (c, tc) in enumerate(tile_groups()):
                    if g % 2:
                        t0, n = TOK[tc]
                        cnd = 1 if tc == 2 else 0
                        dve.wait_ge(ready, g + 1)
                        V_.tensor_scalar(dst[:, c, t0:t0 + n], bank[g % 4][:, 0:n], Ac[:, c, cnd:cnd + 1], Bc[:, c, cnd:cnd + 1],
                                         ALU.mult, ALU.add).then_inc(done, 1)
            leave(hT, A1, sh1, t1_ready, t1_dve)

            dve.wait_ge(pads, 1)
            with dve.Fori(0, 2) as i:
                for jj in range(2):
                    for tc, (t0, n) in enumerate(TOK):
                        m = 3 * jj + tc
                        dve.wait_ge(sg_ok, i * 6 + (m + 1))
                        V_.tensor_tensor(glu[:, ds(i * 2 + jj, 1), GLU_AT[tc]:GLU_AT[tc] + n].rearrange("p a n -> p (a n)"),
                                         bank[2 * tc][:, 0:n], sg[:, m % 2, 0:n], ALU.mult).then_inc(u_free, 1)
            dve.wait_ge(u_free, 15)
            base = steps[0]
            with dve.Fori(0, KC) as k:
                def row(t, off, w):
                    return t[:, ds(k, 1), off:off + w].rearrange("p a n -> p (a n)")
                V_.tensor_scalar(row(conv, 0, CONV_W), row(glu, 0, CONV_W), row(dw, 0, 1),
                                 colv[:, ds(k + CV["dwb"], 1)], ALU.mult, ALU.add).then_inc(chain, 1)
                for t in range(1, TAPS):
                    dve.wait_ge(chain, k * TAPS + (base + t))
                    V_.scalar_tensor_tensor(out=row(conv, 0, CONV_W), in0=row(glu, t, CONV_W), scalar=row(dw, t, 1),
                                            in1=row(conv, 0, CONV_W), op0=ALU.mult, op1=ALU.add).then_inc(chain, 1)
            steps[0] += KC * TAPS
            dve.wait_ge(chain, steps[0])
            V_.memset(marks[:, 4:5], 0.0).then_inc(conv_done, 1)

            for tc, (t0, n) in enumerate(TOK):
                c0 = CONV_AT[tc]
                dve.wait_ge(ln_sum, tc + 1)
                for k in range(KC):
                    V_.scalar_tensor_tensor(out=conv[:, k, c0:c0 + n], in0=bank[0][:, 0:n], scalar=-1.0 / DC,
                                            in1=conv[:, k, c0:c0 + n], op0=ALU.mult, op1=ALU.add).then_inc(ln_mid, 1)
                dve.wait_ge(ln_std, tc + 1)
                link(V_.reciprocal(rs[:, 0:n], rs[:, 0:n]))
                for k in range(KC):
                    V_.tensor_tensor(conv[:, k, c0:c0 + n], conv[:, k, c0:c0 + n], rs[:, 0:n], ALU.mult).then_inc(ln_norm, 1)
            dve.wait_ge(ada_copied, 26)
            link(V_.tensor_tensor(mod[:, 16:48, :], modraw[:, 16:48, :], bcast(CV["bada"] + 16, 32), ALU.add))
            link(V_.scalar_tensor_tensor(out=A2, in0=sc2, scalar=1.0, in1=bcast(CV["n2"], KD), op0=ALU.add, op1=ALU.mult))
            V_.memset(marks[:, 5:6], 0.0).then_inc(mod2_ok, 1)

            SL, SC, TB, OB = (0, 1), (2, 3), (4, 5, 6), 7
            plan = []
            for kind, n in ORDER:
                if kind == "S":
                    plan.append(("M", n))
                if kind == "T":
                    plan.append(("G", GROUPS.index(("P", n, 0))))
                if kind == "V":
                    plan.append(("D", n))
            NL = 3
            base = steps[0]
            with dve.Fori(0, 2) as hh:
                for par in range(2):
                    hp = hh * 2 + par
                    su = hh * (2 * NU) + par * NU
                    link_n = [base]

                    dve.wait_ge(bias_ok, hh * 4 + (2 * par + 2))
                    for kind, n in plan:
                        if kind == "M":
                            u = n
                            _, _, nr, sl, hd = UNITS[u]
                            dve.wait_ge(s_ready, su + (u + 1))
                            if u >= 2:
                                dve.wait_ge(p_ok, su + (u - 1))
                            sc_bank = bank[SC[u % 2]]
                            if nr:
                                w = nr * GRID_W // 2
                                V_.tensor_reduce(mx[:, u % 2, 2:3], sc_bank[:, 0:PAST], AX_X, ALU.max).then_inc(s_part, 1)
                                for b in range(2):
                                    bt = bias[par][hd][0][:, sl - 1:sl - 1 + nr, :] if nr == 8 else bias[par][hd][1]
                                    bt = bt.rearrange("p a n -> p (a n)")[:, b * w:b * w + w]
                                    V_.tensor_tensor_reduce(S[:, u % 2, b * w:b * w + w], bank[SL[b]][:, 0:w], bt, 1.0, MASKED,
                                                            ALU.add, ALU.max, mx[:, u % 2, b:b + 1]).then_inc(s_added if b else s_part, 1)
                                dve.wait_ge(s_added, hh * (2 * LOCAL_UNITS) + (par * LOCAL_UNITS + u + 1))
                                V_.tensor_reduce(nmx[:, u % 2:u % 2 + 1], mx[:, u % 2, 0:3], AX_X, ALU.max, negate=True).then_inc(nmax_ok, 1)
                            else:
                                V_.tensor_reduce(nmx[:, u % 2:u % 2 + 1], sc_bank[:, 0:TP], AX_X, ALU.max, negate=True).then_inc(nmax_ok, 1)
                        if kind == "G":
                            what, m, g = GROUPS[n]
                            dve.wait_ge(tg_ready, hh * (2 * NG) + (par * NG + n + 1))
                            if m >= 2:
                                dve.wait_ge(vv_ready, su + (m - 1))
                            blk = blocks(m)[0]
                            V_.tensor_copy(PT[:, m % 2, 0:P * len(blk)], bank[TB[n % 3]][:, 0:P * len(blk)]).then_inc(tg_dve, 1)
                            dve.wait_ge(p_ok, su + (m + 1))
                            if UNITS[m][2]:
                                V_.tensor_tensor(rsum[:, m % 4:m % 4 + 1], sums[:, m % 4, 0:1], sums[:, m % 4, 1:2], ALU.add).then_inc(sum_ok, 1)
                            else:
                                V_.tensor_copy(rsum[:, m % 4:m % 4 + 1], sums[:, m % 4, 1:2]).then_inc(sum_ok, 1)
                            dve.wait_ge(sum_ok, su + (m + 1))
                            V_.reciprocal(rinv[:, m % 4:m % 4 + 1], rsum[:, m % 4:m % 4 + 1]).then_inc(rinv_ok, 1)
                        if kind == "D" and n % 2:
                            m = n // 2
                            dve.wait_ge(vv_ready, su + (n + 1))
                            dve.wait_ge(rinv_ok, su + (n + 1))
                            if m >= 2:
                                dve.wait_ge(tg_ready, hh * (2 * NG) + (par * NG + GROUPS.index(("O", m - 2, 0)) + 1))
                            for hd in range(2):
                                u = n - 1 + hd
                                last = V_.tensor_scalar(otok[:, m % 2, DH * hd:DH * hd + DH], bank[OB][:, DH * hd:DH * hd + DH],
                                                        rinv[:, u % 4:u % 4 + 1], None, ALU.mult)
                            last.then_inc(o_done, 1)

            with dve.Fori(0, 4) as i:
                for s in range(2):
                    for tc, (t0, n) in enumerate(TOK):
                        m = 3 * s + tc
                        dve.wait_ge(m_sig, i * 12 + 2 * (m + 1))
                        for g in range(2):
                            last = V_.tensor_tensor(mt[:, m % 2, g, 0:n], bank[4 * (m % 2) + 2 + g][:, 0:n], gs[:, m % 2, g, 0:n],
                                                    ALU.mult)
                        last.then_inc(m_free, 1)
                        dve.wait_ge(m_free, i * 6 + (m + 3))
                        V_.tensor_tensor(merged[:, ds(i * 2 + s, 1), t0:t0 + n].rearrange("p a n -> p (a n)"),
                                         mt[:, m % 2, 0, 0:n], mt[:, m % 2, 1, 0:n], ALU.add).then_inc(m_done, 1)

            dve.wait_ge(mod2_ok, 1)
            for cnd in range(2):
                for c in range(KD):
                    n = cnd * KD + c
                    if n >= 2:
                        dve.wait_ge(g1_ps, n - 1)
                    V_.tensor_scalar(diag[:, n % 2, :], ident, g1c[:, c, cnd:cnd + 1], None, ALU.mult).then_inc(g1_diag, 1)
            dve.wait_ge(g1_ok, 4)
            dve.wait_ge(x_in6, 32)
            for n in range(2 * NT):
                t, h = divmod(n, 2)
                cnd = 0 if t < TS // P else 1
                dve.wait_ge(o6_ready, n + 1)
                cols = slice(512 * h, 512 * h + 512)
                V_.tensor_tensor(mt6[:, n % 2, :], bank[n % 4][:, :], g1row[:, cnd, cols], ALU.mult).then_inc(o6_done, 1)
                dve.wait_ge(o6_done, n + 1)
                V_.tensor_tensor(x1[:, t, cols], x1[:, t, cols], mt6[:, n % 2, :], ALU.add).then_inc(x1_ok, 1)
            dve.wait_ge(std6, 1)
            link2 = V_.reciprocal(rstd, std)
            link2.then_inc(rinv6, 1)
            dve.wait_ge(rinv6, 1)
            dve.wait_ge(yacc_out, 16 * NT)
            for t in range(NT):
                V_.tensor_scalar(x1[:, t, :], x1[:, t, :], rstd[:, t:t + 1], None, ALU.mult).then_inc(xs6, 1)
            leave(h2T, A2, sh2, t6_ready, t6_dve)
            rt = [0]

            def rlink(ins):
                rt[0] += 1
                ins.then_inc(router, 1)
                dve.wait_ge(router, rt[0])
            dve.wait_ge(lg_ready, 1)
            lgp = bank[4][:, 0:NT * NE].rearrange("p (t e) -> p t e", e=NE)
            rlink(V_.tensor_reduce(small[:, 0, 0:NT], lgp, AX_X, ALU.max))
            V_.tensor_tensor(lg, lgp, small[:, 0, 0:NT].unsqueeze(2).to_broadcast((P, NT, NE)), ALU.subtract).then_inc(ex_in, 1)
            dve.wait_ge(ex_ok, 1)
            rlink(V_.tensor_reduce(small[:, 1, 0:NT], aff, AX_X, ALU.add))
            rlink(V_.reciprocal(small[:, 2, 0:NT], small[:, 1, 0:NT]))
            V_.tensor_tensor(aff, aff, small[:, 2, 0:NT].unsqueeze(2).to_broadcast((P, NT, NE)), ALU.mult).then_inc(aff_ok, 1)
            dve.wait_ge(aT_ok, 3)
            idx8 = idxu.bitcast(U32)
            for lo, size, cap, v0 in ((0, TS, CAP_S, 0), (TS, TP, CAP_P, CAP_S)):
                src = [affT[0:NE, lo:lo + size], work[0:NE, lo:lo + size]]
                for r in range(cap // 8):
                    v8 = vals[0:NE, v0 + 8 * r:v0 + 8 * r + 8]
                    rlink(V_.max(v8, src[r % 2]))
                    V_.max_index(idx8[0:NE, v0 + 8 * r:v0 + 8 * r + 8], v8, src[r % 2])
                    rlink(V_.match_replace(src[1 - r % 2], v8, src[r % 2], -1.0))
            rlink(V_.tensor_copy(idxf[0:NE, :], idx8[0:NE, :]))
            rlink(V_.tensor_scalar(idxf[0:NE, CAP_S:CAP], idxf[0:NE, CAP_S:CAP], float(TS), None, ALU.add))
            V_.memset(marks[:, 6:7], 0.0).then_inc(topk_ok, 1)
            dve.wait_ge(kt_ready, 1)
            V_.tensor_copy(gT[:, 0, :], bank[5][:, 0:NE])
            V_.tensor_copy(gT[0:CAP_P, 1, :], bank[5][0:CAP_P, NE:2 * NE])
            iTu = iT.rearrange("p a n -> p (a n)").bitcast(U32).rearrange("p (a n) -> p a n", a=2)
            V_.tensor_copy(iTu[:, 0, 0:NE], bank[5][:, 2 * NE:3 * NE])
            V_.tensor_copy(iTu[0:CAP_P, 1, 0:NE], bank[5][0:CAP_P, 3 * NE:4 * NE])
            V_.tensor_copy(iTu[:, 0, NE:NE + 1], bank[5][:, 2 * NE:2 * NE + 1])
            rlink(V_.tensor_copy(iTu[0:CAP_P, 1, NE:NE + 1], bank[5][0:CAP_P, 3 * NE:3 * NE + 1]))
            V_.memset(marks[:, 7:8], 0.0).then_inc(kt_ok, 1)

            gu32, su32 = gidx.bitcast(U32), sidx.bitcast(U32)

            def column(dst, e, done):
                V_.tensor_copy(dst[:, 0:1], iTu[:, 0, ds(e, 1)])
                V_.tensor_copy(dst[0:CAP_P, 1:2], iTu[0:CAP_P, 1, ds(e, 1)]).then_inc(done, 1)

            def xe_leave(e):
                dve.wait_ge(tin_ready, e * 16 + 16)
                for c in range(KD):
                    V_.tensor_scalar(xeT[:, c, CAP_S:CAP], bank[6][:, CAP_P * c:CAP_P * c + CAP_P], A2[:, c, 1:2], sh2[:, c, 1:2],
                                     ALU.mult, ALU.add).then_inc(xe_dve, 1)
            column(gu32, 0, gidx_ok)
            xe_leave(0)
            with dve.Fori(0, NE) as e:
                dve.wait_ge(gathered, e * 32 + 32)
                column(gu32, e + 1, gidx_ok)
                dve.wait_ge(scattered, e * 32)
                column(su32, e, sidx_ok)
                for f in range(KE):
                    dve.wait_ge(silu_ok, e * 16 + (f + 1))
                    V_.tensor_tensor(hid[:, f, :], bank[f % 2][:, CAP:2 * CAP], sil[:, f % 2, :], ALU.mult).then_inc(hid_ok, 1)
                xe_leave(e + 1)
                for h in range(2):
                    dve.wait_ge(tb_ready, e * 2 + (h + 1))
                    V_.tensor_scalar(ye[:, 0, 512 * h:512 * h + 512], bank[4 + h][:, :], gT[:, 0, ds(e, 1)], None, ALU.mult).then_inc(ye_ok, 1)
                    V_.tensor_scalar(ye[0:CAP_P, 1, 512 * h:512 * h + 512], bank[6 + h][0:CAP_P, :], gT[0:CAP_P, 1, ds(e, 1)], None,
                                     ALU.mult).then_inc(ye_ok, 1)
            dve.wait_ge(std8, 1)
            V_.reciprocal(rstd, std).then_inc(rinv6, 1)
            dve.wait_ge(rinv6, 2)
            dve.wait_ge(fg_in, 16)
            for t in range(NT):
                V_.scalar_tensor_tensor(out=yo[:, t, :], in0=yf[:, t, :], scalar=rstd[:, t:t + 1], in1=fgb,
                                        op0=ALU.mult, op1=ALU.mult).then_inc(y_ok, 1)


_OUTS = {"y_prompt": (1, TP, D), "y_sample": (1, TS, D), "state_k": (1, 1, TP, HEADS, DH), "state_v": (1, 1, TP, HEADS, DH)}


def kernel(**inputs):
    import concourse.bacc as bacc
    from concourse.bass_utils import run_bass_kernel_spmd

    nc = bacc.Bacc("TRN2", target_bir_lowering=False, num_devices=1)
    arrays, ins, outs = {}, {}, {}
    inputs["na_rpb"] = inputs["na_rpb"][..., ::-1]
    for name, a in dict(inputs, window_masks=window_masks()).items():
        a = np.ascontiguousarray(a)
        arrays[f"in_{name}"] = a
        ins[name] = nc.dram_tensor(f"in_{name}", a.shape, mybir.dt.from_np(a.dtype), kind="ExternalInput").ap()
    for name, shape in _OUTS.items():
        outs[name] = nc.dram_tensor(f"out_{name}", shape, F32, kind="ExternalOutput").ap()
    backbone(nc, ins, outs)
    r = run_bass_kernel_spmd(nc, [arrays], core_ids=[0])
    return tuple(r.results[0][f"out_{name}"] for name in _OUTS)
```

```python
from contextlib import ExitStack

import numpy as np

import concourse.bass as bass
from concourse import mybir

ALU = mybir.AluOpType
ACT = mybir.ActivationFunctionType
F32 = mybir.dt.float32
F32R = mybir.dt.float32r
U32 = mybir.dt.uint32
AX_X = mybir.AxisListType.X
ds = bass.ds

P = 128
D = 1024
KD = D // P
TS, TP = 1024, 256
T = TS + TP
NT = T // P
GRID_W = 64
ROWS = TS // GRID_W
PAST = 512
DC = 512
KC = DC // P
TAPS = 31
PAD = TAPS // 2
DH = 64
HEADS = 8
NE = 16
DE = 2048
KE = DE // P
CAP_S, CAP_P = 2 * TS // NE, 2 * TP // NE
CAP = CAP_S + CAP_P
EPS = 1e-6
MASKED = -1e30
RPB_R, RPB_C = 15, 31
SLOTS = 14
TOK = [(0, 512), (512, 512), (1024, 256)]
GLU_W = TS + TP + 4 * PAD
GLU_AT = [PAD, PAD + 512, TS + 3 * PAD]
CONV_W = GLU_W - 2 * PAD
CONV_AT = [0, 512, TS + 2 * PAD]
PAIRS = []
for _r in range(0, ROWS, 2):
    _s = min(max(_r - 4, 0), ROWS - 8)
    _s2 = min(max(_r - 3, 0), ROWS - 8)
    PAIRS.append((_s, 8 if _s2 == _s else 9, _s - _r + 7))


def window_masks():
    q = np.arange(P) % GRID_W
    start = np.clip(q - 8, 0, GRID_W - 16)[:, None]
    kc = np.arange(GRID_W)[None, :]
    col = np.where((kc >= start) & (kc < start + 16), 0.0, MASKED).astype(np.float32)
    m = np.repeat(col[:, None, :], 10, axis=1)
    m[GRID_W:, 1, :] = MASKED
    m[:GRID_W, 9, :] = MASKED
    return np.ascontiguousarray(m)


def backbone(nc, A, O):
    ctx = ExitStack()
    with ctx:
        def sem(name):
            return ctx.enter_context(nc.semaphore(name))

        arena_at = -(-nc.sbuf_base // 32) * 32
        arena = ctx.enter_context(nc.sbuf_tensor("arena", [P, 53120], F32))

        def at(off, *dims):
            n = int(np.prod(dims))
            v = arena[:, off:off + n]
            if len(dims) == 1:
                return v
            names = "abcd"[:len(dims)]
            return v.rearrange(f"p ({' '.join(names)}) -> p {' '.join(names)}",
                               **{k: d for k, d in zip(names, dims)})

        def rounded_at(name, off, *dims):
            v = nc.alloc_sbuf_tensor_at(name, [P, int(np.prod(dims))], F32R, offset=arena_at + 4 * off)
            return v[:, :].rearrange("p (a b) -> p a b", a=dims[0])

        bank = [ctx.enter_context(nc.psum_tensor(f"bank{i}", [P, 512], F32)) for i in range(8)]

        HT, CONV, GLU = 0, 10240, 15480
        Q, K, V = 21400, 26520, 31640
        R = 36760
        hT = at(HT, KD, T)
        conv = at(CONV, KC, CONV_W)
        glu = at(GLU, KC, GLU_W)
        qT = at(Q, KC, T)
        kT = at(K, KC, T)
        vtok = at(V, NT, DC)
        xin = at(K, NT, D)
        ws = [at(R + 2048 * i, KD, 256) for i in range(4)]
        sg = at(R + 8192, 2, 512)
        sq = [at(R + 7168, KC, 512), at(R + 2048, KC, 512)]
        rs = at(GLU + 2944, T)
        bias = [[(at(GLU + 2944 * i + 1472 * h, SLOTS, GRID_W), at(GLU + 2944 * i + 1472 * h + 896, 9, GRID_W))
                 for h in range(2)] for i in range(2)]
        kcT = at(R, KC, PAST)
        vc = at(R + 2048, PAST // P, DC)
        S = at(R + 4096, 2, 576)
        Pr = at(R + 5248, 2, 1088)
        PT = at(R + 7424, 2, 1152)
        qz = at(R + 9728, 4, P)
        kraw = at(R + 4096, PAST // P, DC)
        kst = at(R + 6144, 2, DC)
        merged = at(K, KD, T)
        wm = [at(R + 3072 * i, 24, P) for i in range(2)]
        w_up = [rounded_at(f"w_up{i}", R + 6144 + 2048 * i, 16, P) for i in range(2)]
        w_down = [rounded_at(f"w_down{i}", R + 3072 * i, 16, P) for i in range(2)]
        h_up = [rounded_at(f"h_up{q}", GLU + 1024 * q, 2, 512) for q in range(KD // 2)]
        h_down = [rounded_at(f"h_down{q}", HT + 2 * T * q, 2, T) for q in range(KD // 2)]
        wo = at(HT, KD, D)
        wo_up = [rounded_at(f"wo_up{q}", 8192 + 2048 * q, 2, D) for q in range(KD // 2)]
        wo_down = [rounded_at(f"wo_down{q}", HT + 2048 * q, 2, D) for q in range(KD // 2)]
        m_up = [rounded_at(f"m_up{i}", 16384 + 1024 * i, KD, P) for i in range(2)]
        m_down = [rounded_at(f"m_down{i}", 18432 + 1024 * i, KD, P) for i in range(2)]
        x1 = at(R, NT, D)
        g1row = at(20480, 2, D)
        mt6 = at(22528, 2, 512)
        h2T = at(K, KD, T)
        slot = [at(4096 * i, 16, 256) for i in range(6)]
        M7 = 26520
        xeT = at(M7, KD, CAP)
        hid = at(M7 + 1280, KE, CAP)
        yT = at(M7 + 3840, KD, CAP)
        sil = at(M7 + 5120, 2, CAP)
        xg = at(M7 + 5440, 2, D)
        ye = at(M7 + 7488, 2, D)
        yf = at(0, NT, D)
        yo = at(10240, NT, D)
        fgb = at(R, D)

        C = R + 10240
        def const(*dims):
            nonlocal C
            v = at(C, *dims)
            C += int(np.prod(dims))
            return v
        ident, ones = const(P), const(P)
        colv = const(92)
        cs = const(KD, 2)
        modraw, mod = const(48, 2), const(48, 2)
        A1, A2 = const(KD, 2), const(KD, 2)
        dw = const(KC, TAPS)
        wr = const(KD, NE)
        ss, std, rstd = const(NT), const(NT), const(NT)
        eps = const(1)
        small = const(3, 16)
        marks = const(16)
        eps_zero = const(64)
        otok = const(2, P)
        mx, nmx, sums = const(2, 3), const(2), const(4, 2)
        rsum, rinv = const(4), const(4)
        lg, aff = const(NT, NE), const(NT, NE)
        gT, iT = const(2, NE), const(2, NE + 1)
        gidx, sidx = const(2), const(2)
        GP = 2 * 32 + NE
        vals, valsR, idxu = const(P), const(P), const(P)
        idxf, idxfR = const(P), const(P)
        half_off = const(1)
        rows, dwr = at(C, P), at(C + P, DC)
        modrow = at(C + P + DC, 2, 256)
        braw = at(C, 2, SLOTS, GRID_W)
        mask = at(C + 2 * SLOTS * GRID_W, 10, GRID_W)
        gs = [at(GLU + 4096, 2, 512), at(C, 2, 512)]
        diag = at(C + D, 2, P)
        affT = const(T)
        work = at(C, TS // 2)
        aff80 = at(C + TS // 2, 4, GP)
        affT_scr = affT[:, 0:D]
        lgT = affT[0:NE, :]
        C += T
        assert C <= 53120, C
        CV = dict(c=0, ctx=8, n1=16, n2=24, bada=32, dwb=80, lng=84, lnb=88)
        sh1, sc1, g1c, sh2, sc2, g2c = (mod[:, 8 * i:8 * i + 8, :] for i in range(6))

        xhat = nc.dram_tensor("xhat", (T, D), F32, kind="Internal").ap()
        yacc = nc.dram_tensor("yacc", (T, D), F32, kind="Internal").ap()
        RP = 64
        NR = HEADS * RPB_R * RPB_C
        rpbp = nc.dram_tensor("rpbp", (RP + NR + RP,), F32, kind="Internal")
        rpbp_ap = rpbp.ap()

        w_in = A["w_in"][0].rearrange("(k p) n -> p k n", p=P)
        w_ada = A["w_ada"][0].rearrange("(k p) n -> p k n", p=P)
        w_pw = A["w_conv_pw"][0].rearrange("(k p) n -> p k n", p=P)
        w_ao = A["w_attn_o"][0].rearrange("(k p) n -> p k n", p=P)
        w_out = A["w_out"][0].rearrange("(k p) n -> p k n", p=P)
        w_g = A["w_gate_e"][0].rearrange("e (k p) n -> e p k n", p=P)
        w_u = A["w_up_e"][0].rearrange("e (k p) n -> e p k n", p=P)
        w_d = A["w_down_e"][0].rearrange("e (k p) n -> e p k n", p=P)

        rows_in, dwr_in, wr_in, mask_in = (sem(n) for n in ("rows_in", "dwr_in", "wr_in", "mask_in"))
        x_in = [sem(f"x_in{tc}") for tc in range(3)]
        kraw_in, vc_in, fg_in = (sem(n) for n in ("kraw_in", "vc_in", "fg_in"))
        wo_in = [sem(f"wo_in{q}") for q in range(KD // 2)]
        ws_in = [sem(f"ws_in{i}") for i in range(4)]
        wm_in = [sem(f"wm_in{i}") for i in range(2)]
        slot_in = [sem(f"slot_in{i}") for i in range(6)]
        bias_in, b14_ok = sem("bias_in"), sem("b14_ok")
        rpb_zero, rpb_done = sem("rpb_zero"), sem("rpb_done")
        idents = sem("idents")
        pre = sem("pre")
        colv_ok, cs_ok, dw_ok = sem("colv_ok"), sem("cs_ok"), sem("dw_ok")
        ada_ready, ada_row, ada_cols, ada_copied = sem("ada_ready"), sem("ada_row"), sem("ada_cols"), sem("ada_copied")
        mod1_ok, mod2_ok = sem("mod1_ok"), sem("mod2_ok")
        sq1, std1, xs1 = sem("sq1"), sem("std1"), sem("xs1")
        t1_ready, t1_act, t1_dve = sem("t1_ready"), sem("t1_act"), sem("t1_dve")
        h_act, h_dve = sem("h_act"), sem("h_dve")
        pads, u_ready, sg_ok, u_free, qk_free = (sem(n) for n in ("pads", "u_ready", "sg_ok", "u_free", "qk_free"))
        v_ready, v_done = sem("v_ready"), sem("v_done")
        chain = sem("chain")
        conv_done = sem("conv_done")
        kc_ready, kc_done, ks_ready, ks_done = sem("kc_ready"), sem("kc_done"), sem("ks_ready"), sem("ks_done")
        ln_sum, ln_mid, ln_sq, ln_var, ln_std, ln_norm, ln_done = (
            sem(n) for n in ("ln_sum", "ln_mid", "ln_sq", "ln_var", "ln_std", "ln_norm", "ln_done"))
        bias_ok, qz_ok = sem("bias_ok"), sem("qz_ok")
        s_ready, s_added, nmax_ok, p_ok = sem("s_ready"), sem("s_added"), sem("nmax_ok"), sem("p_ok")
        tg_ready, tg_act, tg_dve, o_done = sem("tg_ready"), sem("tg_act"), sem("tg_dve"), sem("o_done")
        m_ready, m_sig, m_done = sem("m_ready"), sem("m_sig"), sem("m_done")
        up6, down6 = sem("up6"), sem("down6")
        wh_ok, wl_ok, hh_ok, hl_ok = sem("wh_ok"), sem("wl_ok"), sem("hh_ok"), sem("hl_ok")
        g1_diag, g1_ps, g1_ok = sem("g1_diag"), sem("g1_ps"), sem("g1_ok")
        o6_ready, o6_done, x1_ok, sq6, std6, xs6 = (sem(n) for n in ("o6_ready", "o6_done", "x1_ok", "sq6", "std6", "xs6"))
        x_in6 = sem("x_in6")
        t6_ready, t6_act, t6_dve = sem("t6_ready"), sem("t6_act"), sem("t6_dve")
        lg_ready, ex_in, ex_ok, aff_ok, aT_ready, aT_ok, topk_ok, kt_ready, kt_ok = (
            sem(n) for n in ("lg_ready", "ex_in", "ex_ok", "aff_ok", "aT_ready", "aT_ok", "topk_ok", "kt_ready", "kt_ok"))
        xhat_out, state_out, y_out = sem("xhat_out"), sem("state_out"), sem("y_out")
        x1_out = [sem(f"x1_out{tc}") for tc in range(3)]
        lgT_ready, lgT_ok = sem("lgT_ready"), sem("lgT_ok")
        gidx_ok, gathered, tin_ready, xe_act, xe_dve = (sem(n) for n in ("gidx_ok", "gathered", "tin_ready", "xe_act", "xe_dve"))
        gu_ready, silu_ok, hid_ok, y_ready, yT_ok = (sem(n) for n in ("gu_ready", "silu_ok", "hid_ok", "y_ready", "yT_ok"))
        tb_ready, ye_ok, sidx_ok, scattered = sem("tb_ready"), sem("ye_ok"), sem("sidx_ok"), sem("scattered")
        sq8, std8, y_ok = sem("sq8"), sem("std8"), sem("y_ok")
        yf_in = [sem(f"yf_in{i}") for i in range(NT // 2)]
        pe_turn, pool_turn = sem("pe_turn"), sem("pool_turn")
        m_free, vv_ready, e_loc, s_part, sum_ok, rinv_ok = (sem(n) for n in ("m_free", "vv_ready", "e_loc", "s_part", "sum_ok", "rinv_ok"))
        rinv6, router, q_ok = sem("rinv6"), sem("router"), sem("q_ok")

        UNITS = []
        for i, (r0, nr, sl) in enumerate(PAIRS):
            UNITS += [(i, r0 * GRID_W, nr, sl, hd) for hd in range(2)]
        for i in range(TP // P):
            UNITS += [(len(PAIRS) + i, TS, 0, 0, hd) for hd in range(2)]
        NU = len(UNITS)
        LOCAL_UNITS = 2 * len(PAIRS)

        def blocks(u):
            qt, tok, nr, _, _ = UNITS[u]
            if nr == 0:
                return [[(b * P, P, ("v", tok // P + b)) for b in range(TP // P)]]
            g = [[(b * P, P, ("v", tok // P + b)) for b in range(4)],
                 [(576 + b * P, P, ("c", b)) for b in range(4)]]
            if nr == 9:
                g.append([(512, GRID_W, ("v", tok // P + 4))])
            return g

        GROUPS = []

        def order():
            out = [("S", 0)]
            for u in range(NU):
                if u + 1 < NU:
                    out.append(("S", u + 1))
                if u >= 1:
                    out.append(("V", u - 1))
                out.append(("T", u))
                if u >= 3 and u % 2:
                    out.append(("O", (u - 3) // 2))
            out += [("V", NU - 1), ("O", NU // 2 - 1)]
            return out

        ORDER = order()
        for kind, n in ORDER:
            if kind == "T":
                GROUPS += [("P", n, g) for g in range(len(blocks(n)))]
            if kind == "O":
                GROUPS.append(("O", n, 0))
        NG = len(GROUPS)
        assert NG % 3 == 0, NG
        BY_DVE = [k == "P" and g == 0 for k, _, g in GROUPS]
        NG_DVE, NG_ACT = sum(BY_DVE), NG - sum(BY_DVE)

        def group_done_at(eng, hh, par, i):
            n = sum(x == BY_DVE[i] for x in BY_DVE[:i + 1])
            if BY_DVE[i]:
                eng.wait_ge(tg_dve, hh * (2 * NG_DVE) + (par * NG_DVE + n))
            else:
                eng.wait_ge(tg_act, hh * (2 * NG_ACT) + (par * NG_ACT + n))

        def groups_before(eng, hh, par):
            eng.wait_ge(tg_dve, hh * (2 * NG_DVE) + par * NG_DVE)
            eng.wait_ge(tg_act, hh * (2 * NG_ACT) + par * NG_ACT)

        block = ctx.enter_context(nc.Block())

        def tile_groups():
            return [(c, tc) for tc in range(3) for c in range(KD)]

        @block.sync
        def _(sp):
            def vec(name, row):
                n = int(np.prod(A[name].shape)) // P
                flat = A[name]
                while len(flat.shape) > 1:
                    flat = flat[0]
                sp.dma_start(rows[row:row + n, :], flat.rearrange("(k p) -> k p", p=P)).then_inc(rows_in, 16)
            for name, key in (("c", "c"), ("c_ctx", "ctx"), ("norm1_g", "n1"), ("norm2_g", "n2"), ("b_ada", "bada"),
                              ("conv_dw_b", "dwb"), ("conv_ln_g", "lng"), ("conv_ln_b", "lnb")):
                vec(name, CV[key])
            sp.dma_start(dwr[0:TAPS, :], A["conv_dw_w"][0]).then_inc(dwr_in, 16)

            def ws_load(s, src, n0, n1):
                sp.dma_start(ws[s][:, :, 0:P], src[:, :, ds(n0, P)]).then_inc(ws_in[s], 16)
                sp.dma_start(ws[s][:, :, P:2 * P], src[:, :, ds(n1, P)]).then_inc(ws_in[s], 16)

            for s in range(4):
                ws_load(s, w_ada, 256 * s, 256 * s + P)
                if s < 3:
                    x_rows = A["x_sample"][0, 512 * s:512 * s + 512] if s < 2 else A["x_prompt"][0]
                    sp.dma_start(xin[:, 4 * s:min(4 * s + 4, NT), :], x_rows.rearrange("(t p) d -> p t d", p=P)).then_inc(x_in[s], 16)
            for s in range(4):
                sp.wait_ge(ada_ready, s + 1)
                ws_load(s, w_ada, 1024 + 256 * s, 1024 + 256 * s + P)
            sp.dma_start(wr, A["w_router"][0].rearrange("(k p) n -> p k n", p=P)).then_inc(wr_in, 16)
            sp.wait_ge(rpb_zero, 1)
            sp.dma_start(rpbp_ap[0:RP].rearrange("(a b) -> a b", a=1), eps_zero[0:1, 0:RP]).then_inc(rpb_done, 16)
            sp.dma_start(rpbp_ap[RP + NR:].rearrange("(a b) -> a b", a=1), eps_zero[0:1, 0:RP]).then_inc(rpb_done, 16)
            sp.dma_start(rpbp_ap[RP:RP + NR].rearrange("(a b) -> a b", a=HEADS),
                         A["na_rpb"][0].rearrange("h r c -> h (r c)")).then_inc(rpb_done, 16)

            for j in range(8):
                sp.wait_ge(ada_ready, 5 + j % 2)
                if j >= 2:
                    sp.wait_ge(u_ready, 6 * (j - 1))
                n0 = 2 * DC * (j // 4) + P * (j % 4)
                ws_load(j % 2, w_in, n0, n0 + DC)
                for a in range(2):
                    n = 8 + 2 * j + a
                    sp.wait_ge(ada_ready, n - 1)
                    ws_load(2 + a, w_ada, 256 * n, 256 * n + P)
            for jj in range(2):
                sp.wait_ge(u_ready, 6 * (7 + jj))
                ws_load(jj, w_in, 2048 + 256 * jj, 2048 + 256 * jj + P)
            sp.wait_ge(dw_ok, 1)
            sp.wait_ge(colv_ok, 1)
            sp.dma_start(mask, A["window_masks"]).then_inc(mask_in, 16)

            def load_bias(hp):
                for h in range(2):
                    for half in range(2):
                        off = RP + (1 - half) * RPB_C + 15 - (GRID_W - 1)
                        src = bass.AP(rpbp, off + (2 * hp + h) * RPB_R * RPB_C,
                                      [[1, GRID_W], [RPB_C, SLOTS], [1, GRID_W]])
                        sp.dma_start(braw[64 * half:64 * half + 64, h, :, :], src).then_inc(bias_in, 16)
            sp.wait_ge(rpb_done, 48)
            sp.wait_ge(ada_copied, 26)
            load_bias(0)
            sp.dma_start(kraw, A["cache_ctx_k"][0, 0].rearrange("(t p) h d -> p t (h d)", p=P)).then_inc(kraw_in, 16)
            sp.wait_ge(ks_done, 2)
            sp.dma_start(O["state_k"][0, 0].rearrange("(t p) h d -> p t (h d)", p=P), kst).then_inc(state_out, 16)
            sp.wait_ge(v_done, 20)
            sp.dma_start(O["state_v"][0, 0].rearrange("(t p) h d -> p t (h d)", p=P), vtok[:, 8:10, :]).then_inc(state_out, 16)
            sp.wait_ge(ln_var, 2)
            sp.dma_start(vc, A["cache_ctx_v"][0, 0].rearrange("(t p) h d -> p t (h d)", p=P)).then_inc(vc_in, 16)
            for hp in range(1, 4):
                sp.wait_ge(b14_ok, 2 * hp)
                load_bias(hp)
            sp.wait_ge(o_done, 4 * NU // 2)
            sp.wait_ge(tg_act, 4 * NG_ACT)
            sp.wait_ge(tg_dve, 4 * NG_DVE)
            sp.wait_ge(state_out, 32)

            def wm_load(s, n0):
                for k0, nk, src in ((0, 8, w_in[:, :, ds(n0 + 2560, P)]), (8, 8, w_in[:, :, ds(n0 + 3584, P)]),
                                    (16, 4, w_pw[:, :, ds(n0, P)]), (20, 4, w_ao[:, :, ds(n0, P)])):
                    sp.dma_start(wm[s][:, k0:k0 + nk, :], src).then_inc(wm_in[s], 16)
            sp.wait_ge(vv_ready, 4 * NU)
            wm_load(0, 0)
            wm_load(1, P)
            for tc in range(3):
                with sp.Fori(0, 3) as i:
                    for s in range(2):
                        sp.wait_ge(m_ready, i * 2 + (8 * tc + s + 1))
                        wm_load(s, i * 256 + (256 + P * s))
                if tc < 2:
                    for s in range(2):
                        sp.wait_ge(m_ready, 8 * tc + 7 + s)
                        wm_load(s, P * s)
            sp.wait_ge(m_ready, 24)
            for q in range(KD // 2):
                sp.dma_start(wo[:, 2 * q:2 * q + 2, :], w_out[:, 2 * q:2 * q + 2, :]).then_inc(wo_in[q], 16)
            sp.wait_ge(m_done, 26)
            sp.dma_start(x1[:, 0:8, :], A["x_sample"][0].rearrange("(t p) d -> p t d", p=P)).then_inc(x_in6, 16)
            sp.dma_start(x1[:, 8:10, :], A["x_prompt"][0].rearrange("(t p) d -> p t d", p=P)).then_inc(x_in6, 16)

            def expert_load(e, c):
                s = (c + 2) % 6
                if c < 8:
                    sp.dma_start(slot[s][:, 0:8, :], w_g[e, :, :, 256 * c:256 * c + 256]).then_inc(slot_in[s], 16)
                    sp.dma_start(slot[s][:, 8:16, :], w_u[e, :, :, 256 * c:256 * c + 256]).then_inc(slot_in[s], 16)
                else:
                    n = 256 * (c - 8)
                    sp.dma_start(slot[s][:, 8:16, :], w_d[e, :, 8:16, n:n + 256]).then_inc(slot_in[s], 16)
                    sp.dma_start(slot[s][:, 0:8, :], w_d[e, :, 0:8, n:n + 256]).then_inc(slot_in[s], 16)

            def x1_store(t):
                sp.wait_ge(x1_ok, 2 * t + 2)
                sp.dma_start(yacc[P * t:P * t + P, :], x1[:, t, :]).then_inc(x1_out[t // 4], 16)

            def xhat_store(t):
                sp.wait_ge(xs6, t + 1)
                sp.dma_start(xhat[P * t:P * t + P, :], x1[:, t, :]).then_inc(xhat_out, 16)
            for t in range(NT):
                x1_store(t)
                if t == 7:
                    for n in range(4):
                        xhat_store(n)
            for c in range(6):
                expert_load(0, c)
            for t in range(4, NT):
                xhat_store(t)
            sp.wait_ge(t6_ready, 24)
            sp.wait_ge(xhat_out, 16 * NT)
            sp.dma_start(fgb, A["final_g"].partition_broadcast(P)).then_inc(fg_in, 16)

            def second_half(e):
                for c in range(6, 12):
                    sp.wait_ge(gu_ready, e * 16 + 2 * (c - 5))
                    expert_load(e, c)
            with sp.Fori(0, NE - 1) as e:
                second_half(e)
                for c in range(6):
                    if c < 2:
                        sp.wait_ge(gu_ready, e * 16 + 2 * (c + 7))
                    else:
                        sp.wait_ge(y_ready, e * 8 + 2 * (c - 1))
                    expert_load(e + 1, c)
            second_half(NE - 1)
            sp.wait_ge(scattered, 32 * NE)
            sp.wait_ge(y_ready, 8 * NE)
            for i in range(NT // 2):
                sp.dma_start(yf[:, 2 * i:2 * i + 2, :],
                             yacc[2 * P * i:2 * P * i + 2 * P, :].rearrange("(t p) d -> p t d", p=P)).then_inc(yf_in[i], 16)
            for t in range(NT):
                dst = O["y_sample"][0, P * t:P * t + P, :] if t < TS // P else O["y_prompt"][0, P * t - TS:P * t - TS + P, :]
                sp.wait_ge(y_ok, t + 1)
                sp.dma_start(dst, yo[:, t, :]).then_inc(y_out, 16)
            sp.wait_ge(y_out, 16 * NT)
            for tc, (_, n) in enumerate(TOK):
                sp.wait_ge(x1_out[tc], 16 * (n // P))

        @block.gpsimd
        def _(pool):
            nc.gpsimd.memset(ident, 0.0).then_inc(idents, 1)
            nc.gpsimd.memset(ones, 1.0).then_inc(idents, 1)
            nc.gpsimd.memset(eps, EPS).then_inc(idents, 1)
            pool.wait_ge(idents, 3)
            nc.gpsimd.affine_select(out=ident, in_=ident, compare_op=ALU.not_equal, fill=1.0, base=0,
                                    pattern=[[-1, P]], channel_multiplier=1).then_inc(idents, 1)
            nc.gpsimd.memset(eps_zero[0:1, :], 0.0).then_inc(rpb_zero, 1)
            nc.gpsimd.memset(glu, 0.0).then_inc(pads, 1)
            pool.wait_ge(conv_done, 1)
            nc.gpsimd.memset(qz, 0.0).then_inc(qz_ok, 1)
            pool.wait_ge(qz_ok, 1)
            pool.wait_ge(qk_free, 15)
            pool.wait_ge(mask_in, 16)
            for hh in range(2):
                for par in range(2):
                    pool.wait_ge(bias_in, hh * 128 + (64 * par + 64))
                    if hh == 0 and par == 1:
                        pool.wait_ge(ln_norm, 12)
                    pool.wait_ge(qz_ok, (2 * hh + par) * NU + 1)
                    for h in range(2):
                        m = mask[:, 0:1, :].to_broadcast((P, SLOTS, GRID_W))
                        nc.gpsimd.tensor_tensor(bias[par][h][0], braw[:, h, :, ::-1], m, ALU.add).then_inc(b14_ok, 1)
                    pool.wait_ge(b14_ok, hh * 4 + (2 * par + 2))
                    for h in range(2):
                        b14, b9 = bias[par][h]
                        nc.gpsimd.tensor_tensor(b9, b14[:, 2:11, :], mask[:, 1:10, :], ALU.add).then_inc(bias_ok, 1)
                    for u in range(NU):
                        qt, _, _, _, hd = UNITS[u]
                        if hh or par or u >= 4:
                            pool.wait_ge(s_ready, (2 * hh + par) * NU + u - 3)
                        if u == 0:
                            pool.wait_ge(bias_ok, hh * 4 + (2 * par + 2))
                        pool.wait_ge(qz_ok, (2 * hh + par) * NU + u + 1)
                        half = slice(64 * hd, 64 * hd + 64)
                        nc.gpsimd.tensor_copy(qz[half, u % 4, :],
                                              qT[half, 2 * hh + par, qt * P:qt * P + P]).then_inc(qz_ok, 1)
            pool.wait_ge(xhat_out, 16 * NT)
            for tc, (_, n) in enumerate(TOK):
                pool.wait_ge(x1_out[tc], 16 * (n // P))

            def gather(e):
                pool.wait_ge(gidx_ok, e + 1)
                if not isinstance(e, int):
                    pool.wait_ge(tin_ready, e * 16)
                pool.sem_inc(pool_turn, 1)
                for i, cap in enumerate((CAP_S, CAP_P)):
                    nc.gpsimd.indirect_dma_start(
                        out=xg[0:cap, i, :], out_offset=None, in_=xhat,
                        in_offset=bass.IndirectOffsetOnAxis(ap=gidx[0:cap, i:i + 1].bitcast(U32), axis=0)).then_inc(gathered, 16)
            gather(0)
            with pool.Fori(0, NE) as e:
                gather(e + 1)
                pool.wait_ge(ye_ok, e * 4 + 4)
                pool.wait_ge(sidx_ok, e + 1)
                pool.sem_inc(pool_turn, 1)
                for i, cap in enumerate((CAP_S, CAP_P)):
                    nc.gpsimd.indirect_dma_start(
                        out=yacc, out_offset=bass.IndirectOffsetOnAxis(ap=sidx[0:cap, i:i + 1].bitcast(U32), axis=0),
                        in_=ye[0:cap, i, :], in_offset=None, compute_op=ALU.add).then_inc(scattered, 16)
                pool.wait_ge(scattered, e * 32 + 32)
            pool.wait_ge(gathered, 32 * (NE + 1))
            pool.wait_ge(scattered, 32 * NE)

        @block.tensor
        def _(pe):
            def mm(out, lhsT, rhs, start, stop):
                return nc.tensor.matmul(out, lhsT, rhs, start=start, stop=stop)

            def tr(out, in_, n):
                return nc.tensor.transpose(out, in_, ident[0:n, 0:n])

            pe.wait_ge(idents, 4)
            pe.wait_ge(rows_in, 16 * 8)
            tr(bank[4][:, 0:92], rows[0:92, :], 92).then_inc(pre, 1)
            pe.wait_ge(dwr_in, 16)
            for k in range(KC):
                last = tr(bank[5][:, 32 * k:32 * k + TAPS], dwr[0:TAPS, P * k:P * k + P], TAPS)
            last.then_inc(pre, 1)
            pe.wait_ge(cs_ok, 2)

            def ada(s, b):
                for k in range(KD):
                    last = mm(bank[b][0:2, 0:256], cs[:, k, :], ws[s][:, k, :], k == 0, k == KD - 1)
                last.then_inc(ada_ready, 1)

            def ada_turn(b, n):
                pe.wait_ge(ada_row, n)
                for half in range(2):
                    last = mm(bank[b][:, 256 + 2 * half:258 + 2 * half], modrow[0:2, b - 6, P * half:P * half + P],
                              ident[0:2, 0:2], True, True)
                last.then_inc(ada_cols, 1)

            def turn(src, tc, scaled, ready, act_done, dve_done, b0):
                t0, n = TOK[tc]
                for g, (c, _) in list(enumerate(tile_groups()))[KD * tc:KD * tc + KD]:
                    if c == 0:
                        pe.wait_ge(scaled, (t0 + n) // P)
                    if g >= 4:
                        pe.wait_ge(dve_done if g % 2 else act_done, (g - 4) // 2 + 1)
                    for t in range(n // P):
                        last = tr(bank[b0 + g % 4][:, P * t:P * t + P], src[:, t0 // P + t, P * c:P * c + P], P)
                    last.then_inc(ready, 1)

            for s in range(8):
                pe.wait_ge(ws_in[s % 4], 32 * (s // 4) + 32)
                pe.wait_ge(ada_copied, s + 1)
                ada(s % 4, 6 + s % 2)
                ada_turn(6 + s % 2, s + 1)
                if 4 <= s < 7:
                    turn(xin, s - 4, xs1, t1_ready, t1_act, t1_dve, 0)

            for half in range(2):
                if half:
                    pe.wait_ge(u_free, 15)
                with pe.Fori(0, 2) as i:
                    for jj in range(2):
                        pe.wait_ge(ws_in[jj], i * 32 + (96 + 64 * half))
                        for tc, (t0, n) in enumerate(TOK):
                            pe.wait_ge(qk_free if half else u_free, i * 6 + (3 * jj + tc + 1))
                            pe.wait_ge(h_act, 4 * (tc + 1))
                            pe.wait_ge(h_dve, 4 * (tc + 1))
                            for h in range(2):
                                for k in range(KD):
                                    last = mm(bank[2 * tc + h][:, 0:n], ws[jj][:, k, P * h:P * h + P], hT[:, k, t0:t0 + n],
                                              k == 0, k == KD - 1)
                                last.then_inc(u_ready, 1)
                            if tc:
                                ada_turn(5 + tc, i * 4 + (8 * half + 2 * jj + tc + 8))
                            if tc < 2:
                                pe.wait_ge(ws_in[2 + tc], i * 64 + (128 * half + 32 * jj + 96))
                                pe.wait_ge(ada_copied, i * 4 + (8 * half + 2 * jj + tc + 9))
                                ada(2 + tc, 6 + tc)
            for n in range(20):
                jj, t = divmod(n, NT)
                if t == 0:
                    pe.wait_ge(ws_in[jj], 32 * 7)
                if n < 6:
                    pe.wait_ge(qk_free, 15)
                else:
                    pe.wait_ge(v_done, n - 5)
                for k in range(KD):
                    last = mm(bank[n % 6][:, 0:256], hT[:, k, P * t:P * t + P], ws[jj][:, k, :], k == 0, k == KD - 1)
                last.then_inc(v_ready, 1)
            pe.wait_ge(v_done, 20)
            pe.wait_ge(conv_done, 1)
            for tc, (t0, n) in enumerate(TOK):
                c0 = CONV_AT[tc]
                for k in range(KC):
                    last = mm(bank[2 * tc][:, 0:n], ones, conv[:, k, c0:c0 + n], k == 0, k == KC - 1)
                last.then_inc(ln_sum, 1)
            pe.wait_ge(ada_copied, 26)
            for t in range(2):
                for h in range(KC):
                    last = tr(bank[6 + t][:, P * h:P * h + P], kT[:, h, TS + P * t:TS + P * t + P], P)
                last.then_inc(ks_ready, 1)
            pe.wait_ge(kraw_in, 16)
            for tc, (t0, n) in enumerate(TOK):
                pe.wait_ge(ln_sq, tc + 1)
                for k in range(KC):
                    last = mm(bank[2 * tc + 1][:, 0:n], ones, sq[tc % 2][:, k, 0:n], k == 0, k == KC - 1)
                last.then_inc(ln_var, 1)
                if tc < 2:
                    for h in (2 * tc, 2 * tc + 1):
                        if h < 2:
                            pe.wait_ge(ks_done, h + 1)
                        else:
                            pe.wait_ge(kc_done, h - 1)
                        for t in range(PAST // P):
                            last = tr(bank[6 + h % 2][:, P * t:P * t + P], kraw[:, t, P * h:P * h + P], P)
                        last.then_inc(kc_ready, 1)

            pe.wait_ge(kc_done, 4)
            pe.wait_ge(ln_mid, 12)
            pe.wait_ge(ln_std, 3)
            pe.wait_ge(vc_in, 16)

            SL, SC, TB, OB = (0, 1), (2, 3), (4, 5, 6), 7

            def head_pair(t, tile_of, hp):
                return t[:, ds(hp, 1), tile_of].rearrange("p a n -> p (a n)")

            with pe.Fori(0, 2) as hh:
                for par in range(2):
                    hp = hh * 2 + par
                    su = hh * (2 * NU) + par * NU
                    sl_ = hh * (2 * LOCAL_UNITS) + par * LOCAL_UNITS
                    gcount = 0
                    for kind, u in ORDER:
                        qt, tok, nr, _, hd = UNITS[min(u, NU - 1)]
                        if kind == "S":
                            pe.wait_ge(qz_ok, su + (u + 2))
                            if u >= 2:
                                pe.wait_ge(p_ok, su + (u - 1))
                            if nr:
                                if u >= 1:
                                    pe.wait_ge(s_added, sl_ + u)
                                w = nr * GRID_W // 2
                                for b in range(2):
                                    mm(bank[SL[b]][:, 0:w], qz[:, u % 4, :], head_pair(kT, slice(tok + b * w, tok + b * w + w), hp), True, True)
                                last = mm(bank[SC[u % 2]][:, 0:PAST], qz[:, u % 4, :], head_pair(kcT, slice(0, PAST), hp), True, True)
                            else:
                                last = mm(bank[SC[u % 2]][:, 0:TP], qz[:, u % 4, :], head_pair(kT, slice(TS, T), hp), True, True)
                            last.then_inc(s_ready, 1)
                        if kind == "T":
                            pe.wait_ge(p_ok, su + (u + 1))
                            for g in blocks(u):
                                if gcount >= 3:
                                    group_done_at(pe, hh, par, gcount - 3)
                                elif gcount == 0 and par:
                                    groups_before(pe, hh, par)
                                if g[0][1] < P:
                                    pe.sem_inc(pe_turn, 1)
                                for b, (col, n, _) in enumerate(g):
                                    last = tr(bank[TB[gcount % 3]][0:n, P * b:P * b + P], Pr[:, u % 2, col:col + n], P)
                                last.then_inc(tg_ready, 1)
                                gcount += 1
                        if kind == "V":
                            g0 = GROUPS.index(("P", u, 0))
                            flat = [(i, b, blk) for i, g in enumerate(blocks(u)) for b, blk in enumerate(g)]
                            if hd == 0:
                                pe.wait_ge(o_done, hh * NU + (par * NU // 2 + u // 2))
                            seen = -1
                            for m, (i, b, (col, n, (src, st))) in enumerate(flat):
                                if i != seen:
                                    group_done_at(pe, hh, par, g0 + i)
                                    seen = i
                                vsrc = vc if src == "c" else vtok
                                last = mm(bank[OB][:, DH * hd:DH * hd + DH], PT[0:n, u % 2, P * (4 * i + b):P * (4 * i + b) + P],
                                          vsrc[0:n, st, ds(hp * P + DH * hd, DH)], m == 0, m == len(flat) - 1)
                            last.then_inc(vv_ready, 1)
                        if kind == "O":
                            pe.wait_ge(o_done, hh * NU + (par * NU // 2 + u + 1))
                            group_done_at(pe, hh, par, gcount - 3)
                            tr(bank[TB[gcount % 3]][:, 0:P], otok[:, u % 2, :], P).then_inc(tg_ready, 1)
                            gcount += 1
                groups_before(pe, hh, 2)

            pe.wait_ge(tg_act, 4 * NG_ACT)
            pe.wait_ge(tg_dve, 4 * NG_DVE)
            for tc, (t0, n) in enumerate(TOK):
                with pe.Fori(0, 4) as i:
                    for s in range(2):
                        pe.wait_ge(wm_in[s], i * 64 + (256 * tc + 64))
                        pe.wait_ge(m_free, i * 2 + (8 * tc + s + 1))
                        for which, k0, src, c0 in ((2, 16, conv, CONV_AT[tc]), (3, 20, qT, t0)):
                            for k in range(KC):
                                mm(bank[4 * s + which][:, 0:n], wm[s][:, k0 + k, :], src[:, k, c0:c0 + n], k == 0, k == KC - 1)
                        pe.wait_ge(wl_ok, i * 2 + (8 * tc + s + 1))
                        pe.wait_ge(hl_ok, 4 * (tc + 1))
                        for which in range(2):
                            out = bank[4 * s + which][:, 0:n]
                            for k in range(KD):
                                w_hi, w_lo = w_up[s][:, 8 * which + k, :], w_down[s][:, 8 * which + k, :]
                                h_hi, h_lo = h_up[k // 2][:, k % 2, 0:n], h_down[k // 2][:, k % 2, t0:t0 + n]
                                mm(out, w_hi, h_hi, k == 0, False)
                                mm(out, w_hi, h_lo, False, False)
                                last = mm(out, w_lo, h_hi, False, k == KD - 1)
                        last.then_inc(m_ready, 1)

            for cnd in range(2):
                for c in range(KD):
                    n = cnd * KD + c
                    pe.wait_ge(g1_diag, n + 1)
                    if c == 0:
                        pe.wait_ge(m_done, 26)
                    last = mm(bank[4 + 2 * cnd + c // 4][:, P * (c % 4):P * (c % 4) + P], ones, diag[:, n % 2, :], True, True)
                    last.then_inc(g1_ps, 1)

            def out_tile(t):
                for h in range(2):
                    n = 2 * t + h
                    if n >= 4:
                        pe.wait_ge(o6_done, n - 3)
                    for k in range(KD):
                        if n == 0 and k % 2 == 0:
                            pe.wait_ge(down6, k // 2 + 3)
                        if t >= 2 and h == 0 and k == 0:
                            pe.wait_ge(down6, t + 5)
                        w_hi, w_lo = (w[k // 2][:, k % 2, 512 * h:512 * h + 512] for w in (wo_up, wo_down))
                        x_hi, x_lo = m_up[t % 2][:, k, :], m_down[t % 2][:, k, :]
                        mm(bank[n % 4][:, :], x_hi, w_hi, k == 0, False)
                        mm(bank[n % 4][:, :], x_lo, w_hi, False, False)
                        last = mm(bank[n % 4][:, :], x_hi, w_lo, False, k == KD - 1)
                    last.then_inc(o6_ready, 1)

            def router_logits(tc):
                t0, n = TOK[tc]
                pe.wait_ge(t6_act, 4 * (tc + 1))
                pe.wait_ge(t6_dve, 4 * (tc + 1))
                pe.wait_ge(o6_done, 17 + tc)
                for k in range(KD):
                    last = mm(bank[tc][0:NE, 0:n], wr[:, k, :], h2T[:, k, t0:t0 + n], k == 0, k == KD - 1)
                last.then_inc(lgT_ready, 1)
            for t in range(8):
                out_tile(t)
            pe.wait_ge(g1_ok, 4)
            turn(x1, 0, xs6, t6_ready, t6_act, t6_dve, 4)
            out_tile(8)
            out_tile(9)
            turn(x1, 1, xs6, t6_ready, t6_act, t6_dve, 4)
            pe.wait_ge(wr_in, 16)
            router_logits(0)
            turn(x1, 2, xs6, t6_ready, t6_act, t6_dve, 4)
            router_logits(1)
            router_logits(2)
            pe.wait_ge(lgT_ok, 3)
            pe.wait_ge(o6_done, 20)
            for t in range(NT):
                last = tr(bank[3][:, NE * t:NE * t + NE], lgT[:, P * t:P * t + P], NE)
            last.then_inc(lg_ready, 1)
            pe.wait_ge(aff_ok, 1)
            for t in range(4):
                last = tr(bank[0][0:GP, P * t:P * t + P], aff80[:, t, :], P)
            last.then_inc(aT_ready, 1)
            pe.wait_ge(topk_ok, 1)
            for i, src in enumerate((vals, valsR, idxf, idxfR)):
                last = tr(bank[5][:, GP * i:GP * i + GP], src[0:GP, :], GP)
            last.then_inc(kt_ready, 1)

            def gathered_in(e, before):
                pe.wait_ge(gathered, 32 * e + 32)
                if before is not None:
                    pe.wait_ge(hid_ok, before * 16 + 16)
                for c in range(KD):
                    tr(bank[4 + c // 4][:, P * (c % 4):P * (c % 4) + P], xg[:, 0, P * c:P * c + P], P).then_inc(tin_ready, 1)
                for c in range(KD):
                    tr(bank[6][:, CAP_P * c:CAP_P * c + CAP_P], xg[0:CAP_P, 1, P * c:P * c + P], CAP_P).then_inc(tin_ready, 1)

            pe.wait_ge(kt_ok, 1)
            gathered_in(0, None)
            with pe.Fori(0, NE) as e:
                pe.wait_ge(xe_act, e * 8 + 8)
                pe.wait_ge(xe_dve, e * 8 + 8)
                for c in range(8):
                    s = (c + 2) % 6
                    pe.wait_ge(slot_in[s], e * 64 + 32 * (c // 6 + 1))
                    for ff in range(2):
                        f = 2 * c + ff
                        if f >= 2:
                            pe.wait_ge(hid_ok, e * 16 + (f - 1))
                        for half in range(2):
                            for k in range(KD):
                                last = mm(bank[f % 2][:, CAP * half:CAP * half + CAP], slot[s][:, 8 * half + k, P * ff:P * ff + P],
                                          xeT[:, k, :], k == 0, k == KD - 1)
                        last.then_inc(gu_ready, 1)
                gathered_in(e + 1, e)
                for c in range(8, 12):
                    s = (c + 2) % 6
                    pe.wait_ge(slot_in[s], e * 64 + 64)
                    for dd in range(2):
                        d = 2 * (c - 8) + dd
                        if d >= 2:
                            pe.wait_ge(yT_ok, e * 8 + (d - 1))
                        for f in range(KE):
                            last = mm(bank[2 + d % 2][:, 0:CAP], slot[s][:, f, P * dd:P * dd + P], hid[:, f, :], f == 0, f == KE - 1)
                        last.then_inc(y_ready, 1)
                pe.wait_ge(xe_act, e * 8 + 16)
                pe.wait_ge(xe_dve, e * 8 + 16)
                for d in range(KD):
                    pe.wait_ge(yT_ok, e * 8 + (d + 1))
                    tr(bank[4 + d // 4][:, P * (d % 4):P * (d % 4) + P], yT[:, d, 0:CAP_S], P)
                    last = tr(bank[6 + d // 4][0:CAP_P, P * (d % 4):P * (d % 4) + P], yT[:, d, CAP_S:CAP], P)
                    if d % 4 == 3:
                        last.then_inc(tb_ready, 1)

        @block.scalar
        def _(act):
            A_ = nc.scalar.activation
            act.wait_ge(colv_ok, 1)
            A_(cs[:, :, 0], colv[:, 0:KD], ACT.Silu).then_inc(cs_ok, 1)
            A_(cs[:, :, 1], colv[:, KD:2 * KD], ACT.Silu).then_inc(cs_ok, 1)

            def ada_row_copy(b, n):
                act.wait_ge(ada_ready, n)
                A_(modrow[0:2, b - 6, :], bank[b][0:2, 0:256], ACT.Copy).then_inc(ada_row, 1)

            def ada_copy(b, n, tile0):
                act.wait_ge(ada_cols, n)
                A_(modraw[:, ds(tile0, 2), :], bank[b][:, 256:260].rearrange("p (a c) -> p a c", c=2), ACT.Copy).then_inc(ada_copied, 1)

            act.wait_ge(u_free, 3)
            for s in range(8):
                ada_row_copy(6 + s % 2, s + 1)
                act.wait_ge(ada_cols, s + 1)
                A_(modraw[:, 2 * s:2 * s + 2, :], bank[6 + s % 2][:, 256:260].rearrange("p (a c) -> p a c", c=2),
                   ACT.Copy).then_inc(ada_copied, 1)
                if s == 3:
                    act.wait_ge(sq1, NT)
                    A_(std, ss, ACT.Sqrt, bias=eps, scale=1.0 / D).then_inc(std1, 1)
                if 4 <= s < 7:
                    for g, (c, tc) in enumerate(tile_groups()):
                        if g % 2 == 0 and tc == s - 4:
                            t0, n = TOK[tc]
                            act.wait_ge(t1_ready, g + 1)
                            A_(hT[:, c, t0:t0 + n], bank[g % 4][:, 0:n], ACT.Copy).then_inc(t1_act, 1)

            def ada_steps(tc, n, tile0):
                if tc:
                    ada_copy(5 + tc, n + tc, tile0 + 2 * (tc - 1))
                if tc < 2:
                    ada_row_copy(6 + tc, n + (tc + 1))

            def leave(dst, tc_, Ac, Bc, ready, done):
                for g, (c, tc) in enumerate(tile_groups()):
                    if g % 2 == 0 and tc == tc_:
                        t0, n = TOK[tc]
                        cnd = 1 if tc == 2 else 0
                        act.wait_ge(ready, g + 1)
                        A_(dst[:, c, t0:t0 + n], bank[4 + g % 4][:, 0:n], ACT.Identity, bias=Bc[:, c, cnd:cnd + 1],
                           scale=Ac[:, c, cnd:cnd + 1]).then_inc(done, 1)
            act.wait_ge(mod1_ok, 1)
            act.wait_ge(t1_act, 12)
            for g, (c, tc) in enumerate(tile_groups()):
                if g % 2 == 0:
                    t0, n = TOK[tc]
                    cnd = 1 if tc == 2 else 0
                    A_(hT[:, c, t0:t0 + n], hT[:, c, t0:t0 + n], ACT.Identity, bias=sh1[:, c, cnd:cnd + 1],
                       scale=A1[:, c, cnd:cnd + 1]).then_inc(h_act, 1)

            with act.Fori(0, 2) as i:
                for jj in range(2):
                    for tc, (t0, n) in enumerate(TOK):
                        m = 3 * jj + tc
                        act.wait_ge(u_ready, i * 12 + 2 * (m + 1))
                        act.wait_ge(u_free, i * 6 + (m + 2))
                        A_(sg[:, m % 2, 0:n], bank[2 * tc + 1][:, 0:n], ACT.Sigmoid).then_inc(sg_ok, 1)
                        ada_steps(tc, i * 4 + (2 * jj + 8), i * 8 + (16 + 4 * jj))
            with act.Fori(0, 2) as i:
                for jj in range(2):
                    for tc, (t0, n) in enumerate(TOK):
                        m = 3 * jj + tc
                        act.wait_ge(u_ready, i * 12 + (24 + 2 * (m + 1)))
                        A_(qT[:, ds(i * 2 + jj, 1), t0:t0 + n].rearrange("p a n -> p (a n)"), bank[2 * tc][:, 0:n], ACT.Copy, scale=DH ** -0.5).then_inc(q_ok, 1)
                        A_(kT[:, ds(i * 2 + jj, 1), t0:t0 + n].rearrange("p a n -> p (a n)"), bank[2 * tc + 1][:, 0:n], ACT.Copy).then_inc(qk_free, 1)
                        ada_steps(tc, i * 4 + (2 * jj + 16), i * 8 + (32 + 4 * jj))
            for n in range(20):
                jj, t = divmod(n, NT)
                act.wait_ge(v_ready, n + 1)
                A_(vtok[:, t, 256 * jj:256 * jj + 256], bank[n % 6][:, 0:256], ACT.Copy).then_inc(v_done, 1)

            def squares(tc):
                t0, n = TOK[tc]
                c0 = CONV_AT[tc]
                act.wait_ge(ln_mid, 4 * (tc + 1))
                A_(sq[tc % 2][:, :, 0:n], conv[:, :, c0:c0 + n], ACT.Square).then_inc(ln_sq, 1)

            def deviation(tc):
                t0, n = TOK[tc]
                act.wait_ge(ln_var, tc + 1)
                A_(rs[:, t0:t0 + n], bank[2 * tc + 1][:, 0:n], ACT.Sqrt, bias=eps, scale=1.0 / DC).then_inc(ln_std, 1)

            def cached_keys(h):
                act.wait_ge(kc_ready, h + 1)
                A_(kcT[:, h, :], bank[6 + h % 2][:, :], ACT.Copy).then_inc(kc_done, 1)
            squares(0)
            for t in range(2):
                act.wait_ge(ks_ready, t + 1)
                A_(kst[:, t, :], bank[6 + t][:, :], ACT.Copy).then_inc(ks_done, 1)
            squares(1)
            cached_keys(0)
            cached_keys(1)
            deviation(0)
            squares(2)
            cached_keys(2)
            cached_keys(3)
            deviation(1)
            deviation(2)
            for tc, (t0, n) in enumerate(TOK):
                c0 = CONV_AT[tc]
                for k in range(KC):
                    act.wait_ge(ln_norm, 4 * tc + k + 1)
                    last = A_(conv[:, k, c0:c0 + n], conv[:, k, c0:c0 + n], ACT.Silu, scale=colv[:, CV["lng"] + k:CV["lng"] + k + 1],
                              bias=colv[:, CV["lnb"] + k:CV["lnb"] + k + 1])
                last.then_inc(ln_done, 1)

            act.wait_ge(state_out, 32)
            SC, TB = (2, 3), (4, 5, 6)
            plan = []
            for kind, n in ORDER:
                if kind == "S" and n >= 0:
                    plan.append(("E", n))
                if kind == "T":
                    plan += [("G", GROUPS.index(("P", n, g))) for g in range(len(blocks(n)))]
                if kind == "O":
                    plan.append(("G", GROUPS.index(("O", n, 0))))
            with act.Fori(0, 2) as hh:
                for par in range(2):
                    hp = hh * 2 + par
                    su = hh * (2 * NU) + par * NU
                    for kind, n in plan:
                        if kind == "E":
                            u = n
                            nr = UNITS[u][2]
                            act.wait_ge(nmax_ok, su + (u + 1))
                            gprev = GROUPS.index(("P", u - 2, len(blocks(u - 2)) - 1)) + 1 if u >= 2 else 0
                            if u >= 4:
                                act.wait_ge(sum_ok, su + (u - 3))
                            if u >= 2:
                                act.wait_ge(tg_ready, hh * (2 * NG) + (par * NG + gprev))
                            if nr:
                                act.wait_ge(s_added, hh * (2 * LOCAL_UNITS) + (par * LOCAL_UNITS + u + 1))
                                A_(Pr[:, u % 2, 0:nr * GRID_W], S[:, u % 2, 0:nr * GRID_W], ACT.Exp, bias=nmx[:, u % 2:u % 2 + 1],
                                   accum_out=sums[:, u % 4, 0:1]).then_inc(e_loc, 1)
                                A_(Pr[:, u % 2, 576:576 + PAST], bank[SC[u % 2]][:, 0:PAST], ACT.Exp, bias=nmx[:, u % 2:u % 2 + 1],
                                   accum_out=sums[:, u % 4, 1:2]).then_inc(p_ok, 1)
                            else:
                                A_(Pr[:, u % 2, 0:TP], bank[SC[u % 2]][:, 0:TP], ACT.Exp, bias=nmx[:, u % 2:u % 2 + 1],
                                   accum_out=sums[:, u % 4, 1:2]).then_inc(p_ok, 1)
                        elif not BY_DVE[n]:
                            what, m, g = GROUPS[n]
                            act.wait_ge(tg_ready, hh * (2 * NG) + (par * NG + n + 1))
                            src = bank[TB[n % 3]]
                            if what == "O":
                                A_(qT[:, ds(hp, 1), P * m:P * m + P].rearrange("p a n -> p (a n)"), src[:, 0:P], ACT.Copy).then_inc(tg_act, 1)
                            else:
                                if m >= 2:
                                    act.wait_ge(vv_ready, su + (m - 1))
                                blk = blocks(m)[g]
                                A_(PT[0:blk[0][1], m % 2, 512 * g:512 * g + P * len(blk)], src[0:blk[0][1], 0:P * len(blk)], ACT.Copy).then_inc(tg_act, 1)

            def weight_hi(s, loads):
                act.wait_ge(wm_in[s], loads)
                A_(w_up[s], wm[s][:, 0:16, :], ACT.Copy).then_inc(wh_ok, 1)

            def sigmoids(s, n, before):
                act.wait_ge(m_ready, before + 1)
                act.wait_ge(m_done, before + 1)
                for g in range(2):
                    A_(gs[s][:, g, 0:n], bank[4 * s + g][:, 0:n], ACT.Sigmoid).then_inc(m_sig, 1)
            act.wait_ge(s_added, 4 * LOCAL_UNITS)
            act.wait_ge(tg_act, 4 * NG_ACT)

            def h_hi(tc):
                t0, n = TOK[tc]
                for q in range(KD // 2):
                    A_(h_up[q][:, :, 0:n], hT[:, 2 * q:2 * q + 2, t0:t0 + n], ACT.Copy).then_inc(hh_ok, 1)
            h_hi(0)
            weight_hi(0, 64)
            weight_hi(1, 64)
            for tc, (t0, n) in enumerate(TOK):
                with act.Fori(0, 3) as i:
                    for s in range(2):
                        sigmoids(s, n, i * 2 + (8 * tc + s))
                        weight_hi(s, i * 64 + (256 * tc + 128))
                sigmoids(0, n, 8 * tc + 6)
                if tc < 2:
                    weight_hi(0, 256 * tc + 320)
                    act.wait_ge(m_ready, 8 * tc + 8)
                    h_hi(tc + 1)
                sigmoids(1, n, 8 * tc + 7)
                if tc < 2:
                    weight_hi(1, 256 * tc + 320)
            def merged_hi(t):
                if t >= 2:
                    act.wait_ge(o6_ready, 2 * t - 2)
                A_(m_up[t % 2], merged[:, :, P * t:P * t + P], ACT.Copy).then_inc(up6, 1)
            act.wait_ge(m_done, 26)
            act.wait_ge(m_ready, 24)
            merged_hi(0)
            merged_hi(1)
            for q in range(KD // 2):
                act.wait_ge(wo_in[q], 16)
                A_(wo_up[q], wo[:, 2 * q:2 * q + 2, :], ACT.Copy).then_inc(up6, 1)
            for cnd in range(2):
                for h in range(2):
                    act.wait_ge(g1_ps, 8 * cnd + 4 * h + 4)
                    A_(g1row[:, cnd, 512 * h:512 * h + 512], bank[4 + 2 * cnd + h][:, :], ACT.Copy).then_inc(g1_ok, 1)
            def norms(tc):
                t0, t1 = TOK[tc][0] // P, sum(TOK[tc]) // P
                for t in range(t0, t1):
                    act.wait_ge(x1_ok, 2 * t + 2)
                    if t:
                        act.wait_ge(sq6, t)
                    A_(affT_scr, x1[:, t, :], ACT.Square, accum_out=ss[:, t:t + 1]).then_inc(sq6, 1)
                    if t + 2 < NT:
                        merged_hi(t + 2)
                act.wait_ge(sq6, t1)
                A_(std[:, t0:t1], ss[:, t0:t1], ACT.Sqrt, bias=eps, scale=1.0 / D).then_inc(std6, 1)

            def logits_copy(tc):
                t0, n = TOK[tc]
                act.wait_ge(lgT_ready, tc + 1)
                A_(lgT[:, t0:t0 + n], bank[tc][0:NE, 0:n], ACT.Copy).then_inc(lgT_ok, 1)
            norms(0)
            norms(1)
            leave(h2T, 0, A2, sh2, t6_ready, t6_act)
            norms(2)
            leave(h2T, 1, A2, sh2, t6_ready, t6_act)
            logits_copy(0)
            leave(h2T, 2, A2, sh2, t6_ready, t6_act)
            logits_copy(1)
            logits_copy(2)
            act.wait_ge(ex_in, 1)
            A_(aff, lg, ACT.Exp).then_inc(ex_ok, 1)
            act.wait_ge(aT_ready, 1)
            A_(affT[0:GP, 0:TS // 2], bank[0][0:GP, :], ACT.Copy).then_inc(aT_ok, 1)

            def xe_leave(e):
                for c in range(KD):
                    act.wait_ge(tin_ready, e * 16 + 8)
                    A_(xeT[:, c, 0:CAP_S], bank[4 + c // 4][:, P * (c % 4):P * (c % 4) + P], ACT.Identity,
                       bias=sh2[:, c, 0:1], scale=A2[:, c, 0:1]).then_inc(xe_act, 1)
            xe_leave(0)
            with act.Fori(0, NE) as e:
                for f in range(KE):
                    act.wait_ge(gu_ready, e * 16 + (f + 1))
                    if f >= 2:
                        act.wait_ge(hid_ok, e * 16 + (f - 1))
                    A_(sil[:, f % 2, :], bank[f % 2][:, 0:CAP], ACT.Silu).then_inc(silu_ok, 1)
                xe_leave(e + 1)
                for d in range(KD):
                    act.wait_ge(y_ready, e * 8 + (d + 1))
                    A_(yT[:, d, 0:CAP_S], bank[2 + d % 2][:, 0:CAP_S], ACT.Copy, scale=g2c[:, d, 0:1])
                    A_(yT[:, d, CAP_S:CAP], bank[2 + d % 2][:, CAP_S:CAP], ACT.Copy, scale=g2c[:, d, 1:2]).then_inc(yT_ok, 1)
            for t in range(NT):
                act.wait_ge(yf_in[t // 2], 16)
                if t:
                    act.wait_ge(sq8, t)
                A_(affT_scr, yf[:, t, :], ACT.Square, accum_out=ss[:, t:t + 1]).then_inc(sq8, 1)
                if t % 2:
                    act.wait_ge(sq8, t + 1)
                    A_(std[:, t - 1:t + 1], ss[:, t - 1:t + 1], ACT.Sqrt, bias=eps, scale=1.0 / D).then_inc(std8, 1)

        @block.vector
        def _(dve):
            V_ = nc.vector
            steps = [0]

            def link(ins):
                steps[0] += 1
                ins.then_inc(chain, 1)
                dve.wait_ge(chain, steps[0])

            V_.memset(marks[:, 0:1], 0.0).then_inc(ada_copied, 2)
            V_.memset(marks[:, 1:2], 0.0).then_inc(u_free, 3)
            V_.memset(marks[:, 2:3], 0.0).then_inc(m_free, 2)
            V_.memset(marks[:, 9:10], 0.0).then_inc(m_done, 2)
            V_.memset(marks[:, 8:9], 0.0).then_inc(qk_free, 3)
            dve.wait_ge(pre, 1)
            V_.tensor_copy(colv, bank[4][:, 0:92]).then_inc(colv_ok, 1)
            dve.wait_ge(pre, 2)
            V_.tensor_copy(dw, bank[5][:, 0:P].rearrange("p (k t) -> p k t", t=32)[:, :, 0:TAPS]).then_inc(dw_ok, 1)
            dve.wait_ge(colv_ok, 1)

            for t in range(NT):
                if t % 4 == 0:
                    dve.wait_ge(x_in[t // 4], 16)
                if t:
                    dve.wait_ge(sq1, t)
                V_.tensor_tensor_reduce(arena[:, R + 8192:R + 8192 + D], xin[:, t, :], xin[:, t, :], 1.0, 0.0,
                                        ALU.mult, ALU.add, ss[:, t:t + 1]).then_inc(sq1, 1)

            def bcast(col, n):
                return colv[:, col:col + n].unsqueeze(2).to_broadcast((P, n, 2))
            dve.wait_ge(std1, 1)
            link(V_.reciprocal(rstd, std))

            def scale_rows(tc):
                t0, n = TOK[tc]
                for t in range(t0 // P, (t0 + n) // P):
                    V_.tensor_scalar(xin[:, t, :], xin[:, t, :], rstd[:, t:t + 1], None, ALU.mult).then_inc(xs1, 1)
            scale_rows(0)
            for tc, (t0, n) in enumerate(TOK):
                if tc < 2:
                    scale_rows(tc + 1)
                for c in range(1, KD, 2):
                    g = KD * tc + c
                    dve.wait_ge(t1_ready, g + 1)
                    V_.tensor_copy(hT[:, c, t0:t0 + n], bank[g % 4][:, 0:n]).then_inc(t1_dve, 1)
            dve.wait_ge(ada_copied, 10)
            link(V_.tensor_tensor(mod[:, 0:16, :], modraw[:, 0:16, :], bcast(CV["bada"], 16), ALU.add))
            link(V_.scalar_tensor_tensor(out=A1, in0=sc1, scalar=1.0, in1=bcast(CV["n1"], KD), op0=ALU.add, op1=ALU.mult))
            V_.memset(marks[:, 3:4], 0.0).then_inc(mod1_ok, 1)
            dve.wait_ge(t1_dve, 12)
            for tc, (t0, n) in enumerate(TOK):
                cnd = 1 if tc == 2 else 0
                for c in range(1, KD, 2):
                    V_.tensor_scalar(hT[:, c, t0:t0 + n], hT[:, c, t0:t0 + n], A1[:, c, cnd:cnd + 1], sh1[:, c, cnd:cnd + 1],
                                     ALU.mult, ALU.add).then_inc(h_dve, 1)

            def leave(dst, tc_, Ac, Bc, ready, done):
                for g, (c, tc) in enumerate(tile_groups()):
                    if g % 2 and tc == tc_:
                        t0, n = TOK[tc]
                        cnd = 1 if tc == 2 else 0
                        dve.wait_ge(ready, g + 1)
                        V_.tensor_scalar(dst[:, c, t0:t0 + n], bank[4 + g % 4][:, 0:n], Ac[:, c, cnd:cnd + 1], Bc[:, c, cnd:cnd + 1],
                                         ALU.mult, ALU.add).then_inc(done, 1)

            dve.wait_ge(pads, 1)
            with dve.Fori(0, 2) as i:
                for jj in range(2):
                    for tc, (t0, n) in enumerate(TOK):
                        m = 3 * jj + tc
                        dve.wait_ge(sg_ok, i * 6 + (m + 1))
                        V_.tensor_tensor(glu[:, ds(i * 2 + jj, 1), GLU_AT[tc]:GLU_AT[tc] + n].rearrange("p a n -> p (a n)"),
                                         bank[2 * tc][:, 0:n], sg[:, m % 2, 0:n], ALU.mult).then_inc(u_free, 1)
            dve.wait_ge(u_free, 15)
            base = steps[0]
            with dve.Fori(0, KC) as k:
                def row(t, off, w):
                    return t[:, ds(k, 1), off:off + w].rearrange("p a n -> p (a n)")
                V_.tensor_scalar(row(conv, 0, CONV_W), row(glu, 0, CONV_W), row(dw, 0, 1),
                                 colv[:, ds(k + CV["dwb"], 1)], ALU.mult, ALU.add).then_inc(chain, 1)
                for t in range(1, TAPS):
                    dve.wait_ge(chain, k * TAPS + (base + t))
                    V_.scalar_tensor_tensor(out=row(conv, 0, CONV_W), in0=row(glu, t, CONV_W), scalar=row(dw, t, 1),
                                            in1=row(conv, 0, CONV_W), op0=ALU.mult, op1=ALU.add).then_inc(chain, 1)
            steps[0] += KC * TAPS
            dve.wait_ge(chain, steps[0])
            V_.memset(marks[:, 4:5], 0.0).then_inc(conv_done, 1)

            for tc, (t0, n) in enumerate(TOK):
                c0 = CONV_AT[tc]
                dve.wait_ge(ln_sum, tc + 1)
                for k in range(KC):
                    V_.scalar_tensor_tensor(out=conv[:, k, c0:c0 + n], in0=bank[2 * tc][:, 0:n], scalar=-1.0 / DC,
                                            in1=conv[:, k, c0:c0 + n], op0=ALU.mult, op1=ALU.add).then_inc(ln_mid, 1)
            for tc, (t0, n) in enumerate(TOK):
                c0 = CONV_AT[tc]
                dve.wait_ge(ln_mid, 4 * (tc + 1))
                dve.wait_ge(ln_sq, tc + 1)
                dve.wait_ge(ln_std, tc + 1)
                link(V_.reciprocal(rs[:, t0:t0 + n], rs[:, t0:t0 + n]))
                for k in range(KC):
                    V_.tensor_tensor(conv[:, k, c0:c0 + n], conv[:, k, c0:c0 + n], rs[:, t0:t0 + n], ALU.mult).then_inc(ln_norm, 1)
            dve.wait_ge(ada_copied, 26)
            link(V_.tensor_tensor(mod[:, 16:48, :], modraw[:, 16:48, :], bcast(CV["bada"] + 16, 32), ALU.add))
            link(V_.scalar_tensor_tensor(out=A2, in0=sc2, scalar=1.0, in1=bcast(CV["n2"], KD), op0=ALU.add, op1=ALU.mult))
            V_.memset(marks[:, 5:6], 0.0).then_inc(mod2_ok, 1)

            SL, SC, TB, OB = (0, 1), (2, 3), (4, 5, 6), 7
            plan = []
            for kind, n in ORDER:
                if kind == "S":
                    plan.append(("M", n))
                if kind == "T":
                    plan.append(("G", GROUPS.index(("P", n, 0))))
                if kind == "V":
                    plan.append(("D", n))
            base = steps[0]
            with dve.Fori(0, 2) as hh:
                for par in range(2):
                    hp = hh * 2 + par
                    su = hh * (2 * NU) + par * NU
                    link_n = [base]

                    dve.wait_ge(bias_ok, hh * 4 + (2 * par + 2))
                    for kind, n in plan:
                        if kind == "M":
                            u = n
                            _, _, nr, sl, hd = UNITS[u]
                            dve.wait_ge(s_ready, su + (u + 1))
                            if u >= 2:
                                dve.wait_ge(p_ok, su + (u - 1))
                            sc_bank = bank[SC[u % 2]]
                            if nr:
                                w = nr * GRID_W // 2
                                V_.tensor_reduce(mx[:, u % 2, 2:3], sc_bank[:, 0:PAST], AX_X, ALU.max).then_inc(s_part, 1)
                                for b in range(2):
                                    bt = bias[par][hd][0][:, sl - 1:sl - 1 + nr, :] if nr == 8 else bias[par][hd][1]
                                    bt = bt.rearrange("p a n -> p (a n)")[:, b * w:b * w + w]
                                    V_.tensor_tensor_reduce(S[:, u % 2, b * w:b * w + w], bank[SL[b]][:, 0:w], bt, 1.0, MASKED,
                                                            ALU.add, ALU.max, mx[:, u % 2, b:b + 1]).then_inc(s_added if b else s_part, 1)
                                dve.wait_ge(s_added, hh * (2 * LOCAL_UNITS) + (par * LOCAL_UNITS + u + 1))
                                V_.tensor_reduce(nmx[:, u % 2:u % 2 + 1], mx[:, u % 2, 0:3], AX_X, ALU.max, negate=True).then_inc(nmax_ok, 1)
                            else:
                                V_.tensor_reduce(nmx[:, u % 2:u % 2 + 1], sc_bank[:, 0:TP], AX_X, ALU.max, negate=True).then_inc(nmax_ok, 1)
                        if kind == "G":
                            what, m, g = GROUPS[n]
                            dve.wait_ge(tg_ready, hh * (2 * NG) + (par * NG + n + 1))
                            if m >= 2:
                                dve.wait_ge(vv_ready, su + (m - 1))
                            blk = blocks(m)[0]
                            V_.tensor_copy(PT[:, m % 2, 0:P * len(blk)], bank[TB[n % 3]][:, 0:P * len(blk)]).then_inc(tg_dve, 1)
                            dve.wait_ge(p_ok, su + (m + 1))
                            if UNITS[m][2]:
                                V_.tensor_tensor(rsum[:, m % 4:m % 4 + 1], sums[:, m % 4, 0:1], sums[:, m % 4, 1:2], ALU.add).then_inc(sum_ok, 1)
                            else:
                                V_.tensor_copy(rsum[:, m % 4:m % 4 + 1], sums[:, m % 4, 1:2]).then_inc(sum_ok, 1)
                            dve.wait_ge(sum_ok, su + (m + 1))
                            V_.reciprocal(rinv[:, m % 4:m % 4 + 1], rsum[:, m % 4:m % 4 + 1]).then_inc(rinv_ok, 1)
                        if kind == "D" and n % 2:
                            m = n // 2
                            dve.wait_ge(vv_ready, su + (n + 1))
                            dve.wait_ge(rinv_ok, su + (n + 1))
                            if m >= 2:
                                dve.wait_ge(tg_ready, hh * (2 * NG) + (par * NG + GROUPS.index(("O", m - 2, 0)) + 1))
                            for hd in range(2):
                                u = n - 1 + hd
                                last = V_.tensor_scalar(otok[:, m % 2, DH * hd:DH * hd + DH], bank[OB][:, DH * hd:DH * hd + DH],
                                                        rinv[:, u % 4:u % 4 + 1], None, ALU.mult)
                            last.then_inc(o_done, 1)

            def weight_lo(s, tiles):
                dve.wait_ge(wh_ok, tiles)
                V_.tensor_tensor(w_down[s], wm[s][:, 0:16, :], w_up[s].bitcast(F32), ALU.subtract).then_inc(wl_ok, 1)

            def gated(s, t0, n, c, before):
                for g in range(2):
                    dve.wait_ge(m_sig, before * 2 + (g + 1))
                    last = V_.tensor_tensor(gs[s][:, g, 0:n], bank[4 * s + 2 + g][:, 0:n], gs[s][:, g, 0:n], ALU.mult)
                last.then_inc(m_free, 1)
                dve.wait_ge(m_free, before + 3)
                V_.tensor_tensor(merged[:, ds(c, 1), t0:t0 + n].rearrange("p a n -> p (a n)"),
                                 gs[s][:, 0, 0:n], gs[s][:, 1, 0:n], ALU.add).then_inc(m_done, 1)

            def h_lo(tc):
                t0, n = TOK[tc]
                for q in range(KD // 2):
                    dve.wait_ge(hh_ok, 4 * tc + q + 1)
                    V_.tensor_tensor(h_down[q][:, :, t0:t0 + n], hT[:, 2 * q:2 * q + 2, t0:t0 + n],
                                     h_up[q][:, :, 0:n].bitcast(F32), ALU.subtract).then_inc(hl_ok, 1)
            h_lo(0)
            weight_lo(0, 1)
            weight_lo(1, 2)
            for tc, (t0, n) in enumerate(TOK):
                with dve.Fori(0, 3) as i:
                    for s in range(2):
                        gated(s, t0, n, i * 2 + s, i * 2 + (8 * tc + s))
                        weight_lo(s, i * 2 + (8 * tc + s + 3))
                gated(0, t0, n, 6, 8 * tc + 6)
                if tc < 2:
                    weight_lo(0, 8 * tc + 9)
                    h_lo(tc + 1)
                gated(1, t0, n, 7, 8 * tc + 7)
                if tc < 2:
                    weight_lo(1, 8 * tc + 10)

            dve.wait_ge(mod2_ok, 1)
            for cnd in range(2):
                for c in range(KD):
                    n = cnd * KD + c
                    if n >= 2:
                        dve.wait_ge(g1_ps, n - 1)
                    V_.tensor_scalar(diag[:, n % 2, :], ident, g1c[:, c, cnd:cnd + 1], None, ALU.mult).then_inc(g1_diag, 1)
            def merged_lo(t):
                if t >= 2:
                    dve.wait_ge(o6_ready, 2 * t - 2)
                dve.wait_ge(up6, t + 1 if t < 2 else t + 5)
                V_.tensor_tensor(m_down[t % 2], merged[:, :, P * t:P * t + P], m_up[t % 2].bitcast(F32), ALU.subtract).then_inc(down6, 1)
            merged_lo(0)
            merged_lo(1)
            for q in range(KD // 2):
                dve.wait_ge(up6, q + 3)
                V_.tensor_tensor(wo_down[q], wo[:, 2 * q:2 * q + 2, :], wo_up[q].bitcast(F32), ALU.subtract).then_inc(down6, 1)
            dve.wait_ge(g1_ok, 4)
            dve.wait_ge(x_in6, 32)

            def residual(t):
                cnd = 0 if t < TS // P else 1
                for h in range(2):
                    n = 2 * t + h
                    dve.wait_ge(o6_ready, n + 1)
                    cols = slice(512 * h, 512 * h + 512)
                    V_.tensor_tensor(mt6[:, n % 2, :], bank[n % 4][:, :], g1row[:, cnd, cols], ALU.mult).then_inc(o6_done, 1)
                    dve.wait_ge(o6_done, n + 1)
                    V_.tensor_tensor(x1[:, t, cols], x1[:, t, cols], mt6[:, n % 2, :], ALU.add).then_inc(x1_ok, 1)
                if t + 2 < NT:
                    merged_lo(t + 2)

            def normalise(tc):
                t0, t1 = TOK[tc][0] // P, sum(TOK[tc]) // P
                dve.wait_ge(std6, tc + 1)
                V_.reciprocal(rstd[:, t0:t1], std[:, t0:t1]).then_inc(rinv6, 1)
                dve.wait_ge(rinv6, tc + 1)
                dve.wait_ge(x1_out[tc], 16 * (t1 - t0))
                for t in range(t0, t1):
                    V_.tensor_scalar(x1[:, t, :], x1[:, t, :], rstd[:, t:t + 1], None, ALU.mult).then_inc(xs6, 1)
            for t in range(5):
                residual(t)
            normalise(0)
            for t in range(5, 8):
                residual(t)
            leave(h2T, 0, A2, sh2, t6_ready, t6_dve)
            residual(8)
            normalise(1)
            residual(9)
            normalise(2)
            leave(h2T, 1, A2, sh2, t6_ready, t6_dve)
            leave(h2T, 2, A2, sh2, t6_ready, t6_dve)
            rt = [0]

            def rlink(ins):
                rt[0] += 1
                ins.then_inc(router, 1)
                dve.wait_ge(router, rt[0])
            V_.memset(aff80, -1.0).then_inc(router, 1)
            V_.memset(half_off[0:32, :], 0.0).then_inc(router, 1)
            V_.memset(half_off[32:64, :], float(TS // 2)).then_inc(router, 1)
            rt[0] += 3
            rlink(V_.memset(half_off[64:GP, :], float(TS)))
            dve.wait_ge(lg_ready, 1)
            lgp = bank[3][:, 0:NT * NE].rearrange("p (t e) -> p t e", e=NE)
            rlink(V_.tensor_reduce(small[:, 0, 0:NT], lgp, AX_X, ALU.max))
            V_.tensor_tensor(lg, lgp, small[:, 0, 0:NT].unsqueeze(2).to_broadcast((P, NT, NE)), ALU.subtract).then_inc(ex_in, 1)
            dve.wait_ge(ex_ok, 1)
            rlink(V_.tensor_reduce(small[:, 1, 0:NT], aff, AX_X, ALU.add))
            rlink(V_.reciprocal(small[:, 2, 0:NT], small[:, 1, 0:NT]))
            for col, t0, n in ((0, 0, 4), (32, 4, 4), (64, 8, 2)):
                last = V_.tensor_tensor(aff80[:, 0:n, col:col + NE], aff[:, t0:t0 + n, :],
                                        small[:, 2, t0:t0 + n].unsqueeze(2).to_broadcast((P, n, NE)), ALU.mult)
            last.then_inc(aff_ok, 1)
            dve.wait_ge(aT_ok, 1)
            idx8 = idxu.bitcast(U32)
            src = [affT[0:GP, 0:TS // 2], work[0:GP, :]]
            for r in range(CAP_S // 8):
                v8 = vals[0:GP, 8 * r:8 * r + 8]
                rlink(V_.max(v8, src[r % 2]))
                V_.max_index(idx8[0:GP, 8 * r:8 * r + 8], v8, src[r % 2])
                if r < CAP_S // 8 - 1:
                    rlink(V_.match_replace(src[1 - r % 2], v8, src[r % 2], -1.0))
            rlink(V_.tensor_copy(valsR[0:GP, :], vals[0:GP, ::-1]))
            V_.tensor_scalar(idxf[0:GP, :], idx8[0:GP, :], half_off[0:GP, :], None, ALU.add)
            V_.tensor_scalar(idxfR[0:GP, :], idx8[0:GP, ::-1], half_off[0:GP, :], None, ALU.add).then_inc(topk_ok, 1)
            dve.wait_ge(kt_ready, 1)
            iTu = iT.rearrange("p a n -> p (a n)").bitcast(U32).rearrange("p (a n) -> p a n", a=2)
            early, late, early_i, late_i = (bank[5][:, GP * i + c:GP * i + c + NE] for i, c in ((0, 0), (1, 32), (2, 0), (3, 32)))
            first, apart = gT[:, 1, :], lg[:, 0, :]
            V_.tensor_copy(lg[:, 1, :], late).then_inc(router, 1)
            V_.tensor_copy(lg[:, 2, :], late_i).then_inc(router, 1)
            rt[0] += 2
            dve.wait_ge(router, rt[0])
            V_.tensor_tensor(gT[:, 0, :], early, lg[:, 1, :], ALU.max).then_inc(router, 1)
            V_.tensor_tensor(first, early, lg[:, 1, :], ALU.is_ge).then_inc(router, 1)
            rt[0] += 2
            rlink(V_.tensor_tensor(apart, early_i, lg[:, 2, :], ALU.subtract))
            rlink(V_.tensor_tensor(apart, apart, first, ALU.mult))
            rlink(V_.tensor_tensor(iTu[:, 0, 0:NE], apart, lg[:, 2, :], ALU.add))
            V_.tensor_copy(gT[0:CAP_P, 1, :], bank[5][0:CAP_P, 64:GP])
            V_.tensor_copy(iTu[0:CAP_P, 1, 0:NE], bank[5][0:CAP_P, 2 * GP + 64:3 * GP])
            V_.tensor_copy(iTu[:, 0, NE:NE + 1], iTu[:, 0, 0:1])
            rlink(V_.tensor_copy(iTu[0:CAP_P, 1, NE:NE + 1], bank[5][0:CAP_P, 2 * GP + 64:2 * GP + 65]))
            V_.memset(marks[:, 7:8], 0.0).then_inc(kt_ok, 1)

            gu32, su32 = gidx.bitcast(U32), sidx.bitcast(U32)

            def column(dst, e, done):
                V_.tensor_copy(dst[:, 0:1], iTu[:, 0, ds(e, 1)])
                V_.tensor_copy(dst[0:CAP_P, 1:2], iTu[0:CAP_P, 1, ds(e, 1)]).then_inc(done, 1)

            def xe_leave(e):
                dve.wait_ge(tin_ready, e * 16 + 16)
                for c in range(KD):
                    V_.tensor_scalar(xeT[:, c, CAP_S:CAP], bank[6][:, CAP_P * c:CAP_P * c + CAP_P], A2[:, c, 1:2], sh2[:, c, 1:2],
                                     ALU.mult, ALU.add).then_inc(xe_dve, 1)
            column(gu32, 0, gidx_ok)
            xe_leave(0)
            with dve.Fori(0, NE) as e:
                dve.wait_ge(gathered, e * 32 + 32)
                column(gu32, e + 1, gidx_ok)
                for f in range(KE):
                    dve.wait_ge(silu_ok, e * 16 + (f + 1))
                    V_.tensor_tensor(hid[:, f, :], bank[f % 2][:, CAP:2 * CAP], sil[:, f % 2, :], ALU.mult).then_inc(hid_ok, 1)
                dve.wait_ge(gathered, e * 32 + 64)
                column(su32, e, sidx_ok)
                xe_leave(e + 1)
                for h in range(2):
                    dve.wait_ge(tb_ready, e * 2 + (h + 1))
                    V_.tensor_scalar(ye[:, 0, 512 * h:512 * h + 512], bank[4 + h][:, :], gT[:, 0, ds(e, 1)], None, ALU.mult).then_inc(ye_ok, 1)
                    V_.tensor_scalar(ye[0:CAP_P, 1, 512 * h:512 * h + 512], bank[6 + h][0:CAP_P, :], gT[0:CAP_P, 1, ds(e, 1)], None,
                                     ALU.mult).then_inc(ye_ok, 1)
            dve.wait_ge(fg_in, 16)
            for t in range(NT):
                if t % 2 == 0:
                    dve.wait_ge(std8, t // 2 + 1)
                    V_.reciprocal(rstd[:, t:t + 2], std[:, t:t + 2]).then_inc(rinv6, 1)
                    dve.wait_ge(rinv6, t // 2 + 4)
                V_.scalar_tensor_tensor(out=yo[:, t, :], in0=yf[:, t, :], scalar=rstd[:, t:t + 1], in1=fgb,
                                        op0=ALU.mult, op1=ALU.mult).then_inc(y_ok, 1)


_OUTS = {"y_prompt": (1, TP, D), "y_sample": (1, TS, D), "state_k": (1, 1, TP, HEADS, DH), "state_v": (1, 1, TP, HEADS, DH)}


def kernel(**inputs):
    import concourse.bacc as bacc
    from concourse.bass_utils import run_bass_kernel_spmd

    nc = bacc.Bacc("TRN2", target_bir_lowering=False, num_devices=1)
    arrays, ins, outs = {}, {}, {}
    inputs["na_rpb"] = inputs["na_rpb"][..., ::-1]
    for name, a in dict(inputs, window_masks=window_masks()).items():
        a = np.ascontiguousarray(a)
        arrays[f"in_{name}"] = a
        ins[name] = nc.dram_tensor(f"in_{name}", a.shape, mybir.dt.from_np(a.dtype), kind="ExternalInput").ap()
    for name, shape in _OUTS.items():
        outs[name] = nc.dram_tensor(f"out_{name}", shape, F32, kind="ExternalOutput").ap()
    backbone(nc, ins, outs)
    r = run_bass_kernel_spmd(nc, [arrays], core_ids=[0])
    return tuple(r.results[0][f"out_{name}"] for name in _OUTS)
```
